# Optimizing a Trainium2 kernel written in Bass

```python
import math
import jax, jax.numpy as jnp
from jax import lax
import numpy as np

D_MODEL = 1024
BATCH = 1
SEQ = 512
DEPTH = 2
DEC_BATCH = 8
DEC_SEQ = 4
PAST_LEN = 1024
PAGE_SIZE = 128

N_META = 16
N_MIXERS = 2
N_MLA_LAYERS = (DEPTH + 1) // 2
N_LRU_LAYERS = DEPTH // 2
N_HEADS = 16
Q_LORA = 384
KV_LORA = 256
QK_NOPE = 64
QK_ROPE = 32
V_HEAD = 64
ROPE_THETA = 10000.0
ATTN_SCALE = (QK_NOPE + QK_ROPE) ** -0.5
Q_BLOCK = 128
LRU_WIDTH = D_MODEL
LRU_BLOCKS = 8
LRU_BLOCK = LRU_WIDTH // LRU_BLOCKS
CONV_W = 4
LRU_C = 8.0
D_FF = ((8 * D_MODEL + 3 * 256 - 1) // (3 * 256)) * 256
ALPHA = (2 * DEPTH) ** 0.25
BETA = (8 * DEPTH) ** -0.25
NORM_EPS = 1e-5

kernel_name = 'hybrid_mla_rglru_decoder_step'

def layer_norm(x, g, b):
    xf = x.astype(jnp.float32)
    mu = jnp.mean(xf, axis=-1, keepdims=True)
    var = jnp.mean(jnp.square(xf - mu), axis=-1, keepdims=True)
    y = (xf - mu) * lax.rsqrt(var + NORM_EPS) * g.astype(jnp.float32) + b.astype(jnp.float32)
    return y.astype(x.dtype)

def rms_norm(x, g):
    xf = x.astype(jnp.float32)
    y = xf * lax.rsqrt(jnp.mean(jnp.square(xf), axis=-1, keepdims=True) + NORM_EPS) * g.astype(jnp.float32)
    return y.astype(x.dtype)

def rope(x, pos):
    half = QK_ROPE // 2
    freqs = ROPE_THETA ** (-jnp.arange(half, dtype=jnp.float32) / half)
    ang = pos.astype(jnp.float32)[:, None] * freqs[None, :]
    cos, sin = jnp.cos(ang), jnp.sin(ang)
    if x.ndim == 4:
        cos, sin = cos[:, None, :], sin[:, None, :]
    xf = x.astype(jnp.float32)
    x1, x2 = xf[..., :half], xf[..., half:]
    out = jnp.concatenate([x1 * cos - x2 * sin, x2 * cos + x1 * sin], axis=-1)
    return out.astype(x.dtype)

def mla_project(x, pos, w_in, q_norm, w_q_up, kv_norm, w_uk):
    B, L, _ = x.shape
    z = x @ w_in
    cq = rms_norm(z[..., :Q_LORA], q_norm)
    ckv = rms_norm(z[..., Q_LORA:Q_LORA + KV_LORA], kv_norm)
    kr = rope(z[..., Q_LORA + KV_LORA:], pos)
    q = (cq @ w_q_up).reshape(B, L, N_HEADS, QK_NOPE + QK_ROPE)
    q_rope = rope(q[..., QK_NOPE:], pos)
    q_lat = jnp.einsum('blhn,chn->blhc', q[..., :QK_NOPE], w_uk)
    return q_lat, q_rope, ckv, kr

def mla_attend(q_lat, q_rope, c_kv, k_rope, q_pos, k_pos):
    s = (jnp.einsum('bqhc,bkc->bhqk', q_lat, c_kv).astype(jnp.float32)
         + jnp.einsum('bqhr,bkr->bhqk', q_rope, k_rope).astype(jnp.float32)) * ATTN_SCALE
    mask = k_pos[None, :] <= q_pos[:, None]
    p = jax.nn.softmax(jnp.where(mask, s, -jnp.inf), axis=-1)
    return jnp.einsum('bhqk,bkc->bqhc', p.astype(c_kv.dtype), c_kv)

def mla_prompt_attention(q_lat, q_rope, c_kv, k_rope):
    B, L = q_lat.shape[:2]
    n_blk = -(-L // Q_BLOCK)
    pad = n_blk * Q_BLOCK - L
    ql = jnp.pad(q_lat, ((0, 0), (0, pad), (0, 0), (0, 0)))
    qr = jnp.pad(q_rope, ((0, 0), (0, pad), (0, 0), (0, 0)))
    ql = ql.reshape(B, n_blk, Q_BLOCK, N_HEADS, KV_LORA).swapaxes(0, 1)
    qr = qr.reshape(B, n_blk, Q_BLOCK, N_HEADS, QK_ROPE).swapaxes(0, 1)
    qpos = jnp.arange(n_blk * Q_BLOCK).reshape(n_blk, Q_BLOCK)
    kpos = jnp.arange(L)
    o = lax.map(lambda a: mla_attend(a[0], a[1], c_kv, k_rope, a[2], kpos), (ql, qr, qpos))
    return o.swapaxes(0, 1).reshape(B, n_blk * Q_BLOCK, N_HEADS, KV_LORA)[:, :L]

def mla_output(o_lat, w_uv, w_o):
    B, L = o_lat.shape[:2]
    v = jnp.einsum('blhc,chv->blhv', o_lat, w_uv).reshape(B, L, N_HEADS * V_HEAD)
    return v @ w_o

def causal_conv(u, buf, w, b):
    L = u.shape[1]
    padded = jnp.concatenate([buf, u], axis=1)
    out = b + sum(padded[:, j:j + L] * w[j] for j in range(CONV_W))
    return out, padded[:, L:]

def rglru(xc, h0, w_a, b_a, w_i, b_i, lam):
    B, L, W = xc.shape
    xf = xc.astype(jnp.float32)
    xb = xf.reshape(B, L, LRU_BLOCKS, LRU_BLOCK)
    r = jax.nn.sigmoid(jnp.einsum('blnk,nkj->blnj', xb, w_a.astype(jnp.float32)).reshape(B, L, W) + b_a.astype(jnp.float32))
    i = jax.nn.sigmoid(jnp.einsum('blnk,nkj->blnj', xb, w_i.astype(jnp.float32)).reshape(B, L, W) + b_i.astype(jnp.float32))
    log_a = -LRU_C * r * jax.nn.softplus(-lam.astype(jnp.float32))
    a = jnp.exp(log_a)
    u = jnp.sqrt(jnp.maximum(-jnp.expm1(2.0 * log_a), 0.0)) * (i * xf)

    def step(h, au):
        h = au[0] * h + au[1]
        return h, h

    hT, hs = lax.scan(step, h0.astype(jnp.float32), (a.swapaxes(0, 1), u.swapaxes(0, 1)))
    return hs.swapaxes(0, 1), hT

def lru_mixer(x, h0, conv_buf, w_in, conv_w, conv_b, w_a, b_a, w_i, b_i, lam, w_o):
    z = x @ w_in
    xr, g = z[..., :LRU_WIDTH], z[..., LRU_WIDTH:]
    xc, new_buf = causal_conv(xr, conv_buf, conv_w, conv_b)
    hs, hT = rglru(xc, h0, w_a, b_a, w_i, b_i, lam)
    y = (hs.astype(x.dtype) * jax.nn.gelu(g)) @ w_o
    return y, hT.astype(x.dtype), new_buf

def swiglu(x, w_gu, w_down):
    z = x @ w_gu
    return (jax.nn.silu(z[..., :D_FF]) * z[..., D_FF:]) @ w_down

def setup_inputs(seed: int = 0) -> dict:
    key = jax.random.key(seed)
    ks = jax.random.split(key, 40)
    n_pages = PAST_LEN // PAGE_SIZE
    n_pool = (DEC_BATCH * n_pages * 5) // 4
    f32 = jnp.float32

    def nrm(k, shape, s):
        return jax.random.normal(k, shape, f32) * s

    perm = jax.random.permutation(ks[0], n_pool)[:DEC_BATCH * n_pages]
    page_table = perm.reshape(DEC_BATCH, n_pages).astype(jnp.int32)
    a_base = jax.random.uniform(ks[1], (N_LRU_LAYERS, LRU_WIDTH), f32, 0.9, 0.999) ** (1.0 / LRU_C)
    lam = jnp.log(a_base) - jnp.log1p(-a_base)
    return {
        'x_prompt': nrm(ks[2], (BATCH, SEQ, D_MODEL), 1.0),
        'x_sample': nrm(ks[3], (DEC_BATCH, DEC_SEQ, D_MODEL), 1.0),
        'cache_latent': nrm(ks[4], (N_MLA_LAYERS, n_pool, PAGE_SIZE, KV_LORA), 1.0),
        'cache_krope': nrm(ks[5], (N_MLA_LAYERS, n_pool, PAGE_SIZE, QK_ROPE), 1.0),
        'page_table': page_table,
        'state_lru_h': nrm(ks[6], (N_LRU_LAYERS, DEC_BATCH, LRU_WIDTH), 0.5),
        'state_conv': nrm(ks[7], (N_LRU_LAYERS, DEC_BATCH, CONV_W - 1, LRU_WIDTH), 1.0),
        'meta_tokens': nrm(ks[8], (N_META, D_MODEL), 1.0),
        'mla_w_in': nrm(ks[9], (N_MLA_LAYERS, D_MODEL, Q_LORA + KV_LORA + QK_ROPE), D_MODEL ** -0.5),
        'mla_q_norm': 1.0 + nrm(ks[10], (N_MLA_LAYERS, Q_LORA), 0.02),
        'mla_w_q_up': nrm(ks[11], (N_MLA_LAYERS, Q_LORA, N_HEADS * (QK_NOPE + QK_ROPE)), Q_LORA ** -0.5),
        'mla_kv_norm': 1.0 + nrm(ks[12], (N_MLA_LAYERS, KV_LORA), 0.02),
        'mla_w_uk': nrm(ks[13], (N_MLA_LAYERS, KV_LORA, N_HEADS, QK_NOPE), KV_LORA ** -0.5),
        'mla_w_uv': nrm(ks[14], (N_MLA_LAYERS, KV_LORA, N_HEADS, V_HEAD), KV_LORA ** -0.5),
        'mla_w_o': nrm(ks[15], (N_MLA_LAYERS, N_HEADS * V_HEAD, D_MODEL), BETA * (N_HEADS * V_HEAD) ** -0.5),
        'lru_w_in': nrm(ks[16], (N_LRU_LAYERS, D_MODEL, 2 * LRU_WIDTH), D_MODEL ** -0.5),
        'lru_conv_w': nrm(ks[17], (N_LRU_LAYERS, CONV_W, LRU_WIDTH), CONV_W ** -0.5),
        'lru_conv_b': nrm(ks[18], (N_LRU_LAYERS, LRU_WIDTH), 0.02),
        'lru_w_a': nrm(ks[19], (N_LRU_LAYERS, LRU_BLOCKS, LRU_BLOCK, LRU_BLOCK), LRU_BLOCK ** -0.5),
        'lru_b_a': nrm(ks[20], (N_LRU_LAYERS, LRU_WIDTH), 0.02),
        'lru_w_i': nrm(ks[21], (N_LRU_LAYERS, LRU_BLOCKS, LRU_BLOCK, LRU_BLOCK), LRU_BLOCK ** -0.5),
        'lru_b_i': nrm(ks[22], (N_LRU_LAYERS, LRU_WIDTH), 0.02),
        'lru_lambda': lam,
        'lru_w_o': nrm(ks[23], (N_LRU_LAYERS, LRU_WIDTH, D_MODEL), BETA * LRU_WIDTH ** -0.5),
        'ffn_w_gu': nrm(ks[24], (DEPTH, D_MODEL, 2 * D_FF), D_MODEL ** -0.5),
        'ffn_w_down': nrm(ks[25], (DEPTH, D_FF, D_MODEL), BETA * D_FF ** -0.5),
        'ln_g': 1.0 + nrm(ks[26], (DEPTH, 2, D_MODEL), 0.02),
        'ln_b': nrm(ks[27], (DEPTH, 2, D_MODEL), 0.02),
    }

def reference(x_prompt, x_sample, cache_latent, cache_krope, page_table, state_lru_h, state_conv, meta_tokens,
              mla_w_in, mla_q_norm, mla_w_q_up, mla_kv_norm, mla_w_uk, mla_w_uv, mla_w_o,
              lru_w_in, lru_conv_w, lru_conv_b, lru_w_a, lru_b_a, lru_w_i, lru_b_i, lru_lambda, lru_w_o,
              ffn_w_gu, ffn_w_down, ln_g, ln_b):
    Bp = x_prompt.shape[0]
    Bs, T = x_sample.shape[:2]
    past_len = page_table.shape[1] * cache_latent.shape[2]

    meta = jnp.broadcast_to(meta_tokens[None].astype(x_prompt.dtype), (Bp, N_META, D_MODEL))
    xp = jnp.concatenate([meta, x_prompt], axis=1)
    xs = x_sample
    Lp = xp.shape[1]
    pos_p = jnp.arange(Lp)
    pos_s = past_len + jnp.arange(T)
    kpos_s = jnp.arange(past_len + T)

    lat_p, kr_p, lat_s, kr_s = [], [], [], []
    hp_l, cp_l, hs_l, cs_l = [], [], [], []

    for i in range(DEPTH):
        if i % N_MIXERS == 0:
            a = i // N_MIXERS
            ql, qr, c, kr = mla_project(xp, pos_p, mla_w_in[a], mla_q_norm[a], mla_w_q_up[a], mla_kv_norm[a], mla_w_uk[a])
            mp = mla_output(mla_prompt_attention(ql, qr, c, kr), mla_w_uv[a], mla_w_o[a])
            lat_p.append(c)
            kr_p.append(kr)
            ql, qr, c, kr = mla_project(xs, pos_s, mla_w_in[a], mla_q_norm[a], mla_w_q_up[a], mla_kv_norm[a], mla_w_uk[a])
            c_past = cache_latent[a][page_table].reshape(Bs, past_len, KV_LORA)
            kr_past = cache_krope[a][page_table].reshape(Bs, past_len, QK_ROPE)
            c_all = jnp.concatenate([c_past.astype(c.dtype), c], axis=1)
            kr_all = jnp.concatenate([kr_past.astype(kr.dtype), kr], axis=1)
            ms = mla_output(mla_attend(ql, qr, c_all, kr_all, pos_s, kpos_s), mla_w_uv[a], mla_w_o[a])
            lat_s.append(c)
            kr_s.append(kr)
        else:
            b = i // N_MIXERS
            lw = (lru_w_in[b], lru_conv_w[b], lru_conv_b[b], lru_w_a[b], lru_b_a[b], lru_w_i[b], lru_b_i[b], lru_lambda[b], lru_w_o[b])
            h0 = jnp.zeros((Bp, LRU_WIDTH), xp.dtype)
            buf0 = jnp.zeros((Bp, CONV_W - 1, LRU_WIDTH), xp.dtype)
            mp, hT, bufT = lru_mixer(xp, h0, buf0, *lw)
            hp_l.append(hT)
            cp_l.append(bufT)
            ms, hT, bufT = lru_mixer(xs, state_lru_h[b].astype(xs.dtype), state_conv[b].astype(xs.dtype), *lw)
            hs_l.append(hT)
            cs_l.append(bufT)
        xp = layer_norm(ALPHA * xp + mp, ln_g[i, 0], ln_b[i, 0])
        xs = layer_norm(ALPHA * xs + ms, ln_g[i, 0], ln_b[i, 0])
        xp = layer_norm(ALPHA * xp + swiglu(xp, ffn_w_gu[i], ffn_w_down[i]), ln_g[i, 1], ln_b[i, 1])
        xs = layer_norm(ALPHA * xs + swiglu(xs, ffn_w_gu[i], ffn_w_down[i]), ln_g[i, 1], ln_b[i, 1])

    y_prompt = xp[:, N_META:]
    y_sample = xs
    return (y_prompt, y_sample,
            jnp.stack(lat_p), jnp.stack(kr_p), jnp.stack(lat_s), jnp.stack(kr_s),
            jnp.stack(hp_l), jnp.stack(cp_l), jnp.stack(hs_l), jnp.stack(cs_l))


_drawn_inputs = setup_inputs


def setup_inputs(seed=0):
    import zlib

    import numpy as np

    out = dict(_drawn_inputs(seed))
    spreads = {}
    factors = {'cache_latent': 2.924,
     'cache_krope': 5.466,
     'mla_q_norm': 8.0,
     'mla_kv_norm': 2.979,
     'lru_b_a': 8.0,
     'lru_b_i': 7.954}
    for name, (base, spread) in spreads.items():
        noise = np.random.default_rng([zlib.crc32(name.encode()), seed]).standard_normal(out[name].shape)
        drawn = base * np.exp(spread * noise) if base else spread * noise
        out[name] = __import__('jax').numpy.asarray(drawn.astype(out[name].dtype))
    for name, factor in factors.items():
        out[name] = (out[name] * factor).astype(out[name].dtype)
    return out
```

```python
from contextlib import ExitStack

import numpy as np

import concourse.bass as bass
from concourse import mybir

F32 = mybir.dt.float32
F32R = mybir.dt.float32r
BF16 = mybir.dt.bfloat16
I32 = mybir.dt.int32
ALU = mybir.AluOpType
ACT = mybir.ActivationFunctionType
AX = mybir.AxisListType

P = 128
D = 1024
KD = D // P
SEQ, META = 512, 16
NP = SEQ + META
B, TS = 8, 4
NS = B * TS
T = NP + NS
TH = T // 2
HEADS, NOPE, ROPE, VH = 16, 64, 32, 64
QL_R, KV_R = 384, 256
KQ, KC = QL_R // P, KV_R // P
PAST, PAGE = 1024, 128
PAGES = PAST // PAGE
ROWS = HEADS * TS
FF = 2816
FT = FF // P
FH = FT // 2
CONV = 4
ALPHA = (2 * 2) ** 0.25
SCALE = (NOPE + ROPE) ** -0.5
EPS = 1e-5
LRU_C = 8.0
EARLY = 4
NEG = -1.0e30
PR_AT = (0, 128, 384, 768, 1280, 1808)
XR = T // 5
UP = 3 + NP
UL = UP + B * (3 + TS)

V_G, V_B, V_CW = 0, 32, 64
V_CB, V_BA, V_BI, V_LAM, V_QN, V_KN = 96, 104, 112, 120, 128, 131
NV = 133

C_IN = 0
C_WO = 3
C_FF0 = 7
C_LRU = 37
C_LO = 45
C_FF1 = 49
C_END = 79
W_MAX = FH * 2 * P
W_D = KD * 2 * P
W_LRU = W_D + 2 * P


def chunk_cols(c):
    if C_LRU <= c < C_LO:
        return W_LRU
    for base in (C_FF0, C_FF1):
        if base <= c < base + 30 and (c - base) % 15 >= FH:
            return W_MAX
    return W_D


def chunk_loop(eng, base, n, body, head=0, tail=1):
    pairs = (n - head - tail) // 2
    for j in range(head):
        body(base + j, j, (base + j) // 2, (base + j) % 2)
    if pairs == 1:
        for j in range(head, head + 2):
            body(base + j, j, (base + j) // 2, (base + j) % 2)
    elif pairs > 1:
        with eng.Fori(0, pairs) as i:
            for s in range(2):
                first = base + head + s
                body(i * 2 + first, i * 2 + (head + s), i + first // 2, first % 2)
    for j in range(head + 2 * pairs, n):
        body(base + j, j, (base + j) // 2, (base + j) % 2)


def above_zero(v):
    return not isinstance(v, int) or v > 0


def trunk(nc, x_prompt, x_sample, cache_latent, cache_krope, page_table, state_lru_h, state_conv, meta_tokens,
          mla_w_in, mla_q_norm, mla_w_q_up, mla_kv_norm, mla_w_uk, mla_w_uv, mla_w_o,
          lru_w_in, lru_conv_w, lru_conv_b, lru_w_a, lru_b_a, lru_w_i, lru_b_i, lru_lambda, lru_w_o,
          ffn_w_gu, ffn_w_down, ln_g, ln_b, c_ident, c_trig, c_mask, c_smask,
          y_prompt, y_sample, latent_prompt, krope_prompt, latent_sample, krope_sample,
          h_prompt, conv_prompt, h_sample, conv_sample):
    N_POOL = cache_latent.shape[1]
    with ExitStack() as ctx:
        top = [(nc.sbuf_base + 63) // 64 * 64]

        def place(name, shape, dt, at):
            size = int(np.prod(shape[1:])) * (2 if dt == BF16 else 4)
            return nc.alloc_sbuf_tensor_at(name, shape, dt, offset=at), at + (size + 31) // 32 * 32

        def sb(name, shape, dt=F32):
            t, top[0] = place(name, shape, dt, top[0])
            return t

        def area(at, end):
            pos = [at]

            def put(name, shape, dt=F32):
                t, pos[0] = place(name, shape, dt, pos[0])
                assert pos[0] <= end, (name, pos[0], end)
                return t
            put.at = lambda: pos[0]
            return put

        xT = sb("xT", [P, KD, T])
        xh = sb("xh", [P, KD, T], F32R)
        xl = sb("xl", [P, KD, T], F32R)
        raw = [sb(f"raw{s}", [P, W_MAX]) for s in range(2)]
        ident = sb("ident", [P, P])
        ones = sb("ones", [P, 4, P])
        identb = sb("identb", [P, P], BF16)
        maskb = sb("maskb", [P, P], BF16)
        smaskb = sb("smaskb", [P, B, NS], BF16)
        vec = sb("vec", [P, NV])
        spare = sb("spare", [P, 1])
        hvec = sb("hvec", [P, 16])
        cdec = sb("cdec", [P, 2, KD])
        stT = sb("stT", [P, KD, 32])
        stat = sb("stat", [P, 2, T])
        ring_at = top[0]
        wh = [sb(f"wh{s}", [P, W_MAX], F32R) for s in range(2)]
        wl = [sb(f"wl{s}", [P, W_MAX], F32R) for s in range(2)]
        ring_end = top[0]
        reg = top[0]
        LIMIT = nc.sbuf_top

        put = area(reg, LIMIT)
        z = put("z", [P, KQ + KC, T])
        krs = put("krs", [P, T])
        trig = put("trig", [P, T])
        pages = put("pages", [1, B * PAGES], I32)
        wuv = put("wuv", [P, KC, HEADS * VH])
        wq = [put(f"wq{s}", [P, KQ, P]) for s in range(2)]
        wuk = put("wuk", [P, KC, P])
        heads_at = put.at()
        K = [put(f"K{s}", [P, NP]) for s in range(2)]
        Q = [put(f"Q{s}", [P, T]) for s in range(2)]
        rt = put("rt", [32, 2, T])
        Vs = [put(f"Vs{s}", [P, 5, VH]) for s in range(2)]
        assert put.at() - heads_at >= 4 * PAGES * (KV_R + 2 * ROPE)
        lat = [put(f"lat{s}", [P, KV_R + ROPE]) for s in range(2)]
        cnew = put("cnew", [NS, KV_R + ROPE])
        late_at = reg + 50000
        qlat = put("qlat", [P, KC, B, HEADS, TS])
        qrot = put("qrot", [P, B, HEADS, TS])
        wukT = [put(f"wukT{s}", [NOPE, KV_R]) for s in range(2)]
        mx = put("mx", [P, 2])
        rsum = put("rsum", [P, 4])
        Ctok = [put(f"Ctok{s}", [P, PAGES, KV_R + 2 * ROPE]) for s in range(2)]
        Ctok.append(area(heads_at, LIMIT)("Ctok2", [P, PAGES, KV_R + 2 * ROPE]))
        OL = put("OL", [P, KC, HEADS, B, TS])
        put = area(LIMIT - 28672, LIMIT)
        xin = put("xin", [XR, 5, D])
        prow = put("prow", [P, 2, P])
        srow = put("srow", [32, D])
        cst = put("cst", [P, P + B * NS])
        spt = put("spt", [P, 6, KD])
        put = area(ring_at, ring_end)
        zsq = put("zsq", [P, KQ + KC, T])
        put = area(ring_at, ring_end)
        V = put("V", [P, 5, HEADS * VH])
        Pr = [put(f"Pr{s}", [P, PR_AT[5]]) for s in range(2)]
        PT = put("PT", [P, 4, NP])
        PT4 = put("PT4", [META, META])
        put = area(ring_at, ring_at + 4 * W_MAX)
        CT = put("CT", [P, KC, PAST])
        qs = [put(f"qs{s}", [P, KC, ROWS]) for s in range(3)]
        qrs = [put(f"qrs{s}", [P, ROWS]) for s in range(3)]
        PTn = put("PTn", [NS, ROWS])
        put = area(ring_at + 8 * W_MAX, ring_at + 12 * W_MAX)
        CTR = put("CTR", [P, PAST])
        Ps = put("Ps", [P, PAST + NS])
        PTs = put("PTs", [P, PAGES, ROWS])
        put = area(reg, LIMIT)
        hh = put("hh", [P, FH, T], F32R)
        hl = put("hl", [P, FH, T], F32R)
        sg = [put(f"sg{s}", [P, T]) for s in range(2)]
        ht = [put(f"ht{s}", [P, T]) for s in range(2)]
        sq = [put(f"sq{s}", [P, T]) for s in range(2)]
        ssq = put("ssq", [P, T])
        acc = put("acc", [P, T])
        put = area(reg, LIMIT)
        yh = put("yh", [P, KD, T], F32R)
        yl = put("yl", [P, KD, T], F32R)
        U = [put(f"U{s}", [P, UL]) for s in range(2)]
        gel = [put(f"gel{s}", [P, T]) for s in range(2)]
        th = [put(f"th{s}", [P, T]) for s in range(2)]
        av = [put(f"av{s}", [P, T]) for s in range(2)]
        ix = [put(f"ix{s}", [P, T]) for s in range(2)]
        xc = put("xc", [P, UL])
        xch = put("xch", [P, T], F32R)
        xcl = put("xcl", [P, T], F32R)
        hs = put("hs", [P, NP])
        hist = put("hist", [P, KD, 36])
        as2 = put("as2", [P, B, TS + 1])
        us2 = put("us2", [P, B, TS + 1])
        h2 = put("h2", [P, B, TS + 1])
        gr = [put(f"gr{s}", [P, 2, T]) for s in range(2)]
        put = area(LIMIT - 4160, LIMIT)
        hrow = put("hrow", [36, D])
        put = area(reg, LIMIT)
        yrow = [put(f"yrow{s}", [P, D]) for s in range(2)]

        ps = ctx.enter_context(nc.psum_tensor("ps", [P, 8 * 512], F32))

        def pair(j, lo=0, hi=P):
            return ps[lo:hi, 1024 * j:1024 * j + 1024].rearrange("p (h c) -> p h c", h=2)[:, :, 0:TH]

        def halves(ap):
            return ap.rearrange("p (h c) -> p h c", h=2)

        def samples_of(t):
            return t[:, UP:UL].rearrange("p (b s) -> p b s", b=B)[:, :, 0:TS]

        def sem(name):
            return ctx.enter_context(nc.semaphore(name))

        raw_in = [sem("raw_in0"), sem("raw_in1")]
        hi_ok, lo_ok = sem("hi_ok"), sem("lo_ok")
        t0_ok, t1_ok = sem("t0_ok"), sem("t1_ok")
        f0_ok, f1_ok = sem("f0_ok"), sem("f1_ok")
        in_x = [sem(f"in_x{t}") for t in range(5)]
        in_id, in_par, in_st, in_cst, in_att = (sem(n) for n in ("in_id", "in_par", "in_st", "in_cst", "in_att"))
        in_pg = sem("in_pg")
        s_ones, s_xt, s_xe, s_xh0 = (sem(n) for n in ("ones_ok", "x_turned", "x_read", "x_hi"))
        s_pt_, s_pte, s_stt, s_ste = (sem(n) for n in ("par_turned", "par_read", "st_turned", "st_read"))
        s_par, s_parA, s_cb = sem("par_step"), sem("par_act"), sem("masks_ok")
        s_zsq, s_zms, s_zeps, s_zroot, s_zinv, s_z, s_kr, s_kp2 = (sem(n) for n in (
            "z_sq", "z_ms", "z_eps", "z_root", "z_inv", "z_ok", "kr_step", "k_rope"))
        s_lt, s_lte, s_lout = sem("lat_turned"), sem("lat_read"), [sem(f"lat_out{s}") for s in range(3)]
        s_v, s_ve, s_vd = sem("v_sum"), sem("v_act"), sem("v_dve")
        wq_in, wuk_in = [sem("wq_in0"), sem("wq_in1")], sem("wuk_in")
        wq_sw, v_cp, q_sum, q_act, q_dve, q_rot = (sem(n) for n in ("wq_sw", "v_cp", "q_sum", "q_act", "q_dve", "q_rot"))
        k_sum, k_act, k_dve = sem("k_sum"), sem("k_act"), sem("k_dve")
        wt_sum, wt_rd, ql_sum, ql_rd = (sem(n) for n in ("wt_sum", "wt_rd", "ql_sum", "ql_rd"))
        sc_sum, sc_max, sc_exp, sc_inv, sc_nrm, pt_sum, pt_rd = (sem(n) for n in (
            "sc_sum", "sc_max", "sc_exp", "sc_inv", "sc_nrm", "pt_sum", "pt_rd"))
        o_sum, o_hi, o_lo = sem("o_sum"), sem("o_hi"), sem("o_lo")
        pg_in = [sem(f"pg_in{s}") for s in range(3)]
        d_q, d_fill, d_fa, d_fd, d_s, d_max, d_exp, d_inv, d_nrm = (sem(n) for n in (
            "d_q", "d_fill", "d_fa", "d_fd", "d_s", "d_max", "d_exp", "d_inv", "d_nrm"))
        d_pt, d_pa, d_pd, d_o, d_oa, d_od, d_v, d_vh, d_vl = (sem(n) for n in (
            "d_pt", "d_pa", "d_pd", "d_o", "d_oa", "d_od", "d_v", "d_vh", "d_vl"))
        n_acc, n_mean, n_dev, n_sq, n_var, n_eps, n_root, n_inv = (sem(n) for n in (
            "n_acc", "n_mean", "n_dev", "n_sq", "n_var", "n_eps", "n_root", "n_inv"))
        n_ssq, n_rest, n_rcp, n_rsq, n_ctr, n_ctrp = (sem(n) for n in ("n_ssq", "n_rest", "n_rcp", "n_rsq", "n_ctr", "n_ctrp"))
        n_t, n_hi, n_lo, n_x = (sem(n) for n in ("n_t", "n_hi", "n_lo", "n_x"))
        m_h, m_l = sem("m_h"), sem("m_l")
        r_pad, r_x0, r_cv, r_xh, r_xl, r_g, r_ge, r_ix, r_a, r_th, r_a2, r_v, r_sq = (
            sem("r_" + n) for n in "pad x0 cv xh xl g ge ix a th a2 v sq".split())
        r_u, r_sm, r_s, r_s2, r_y, r_yh, r_yl, r_hc, r_hh, r_z, r_t, r_te = (
            sem("r_" + n) for n in "u sm s s2 y yh yl hc hh z t te".split())
        r_out = sem("r_out")
        y_t, y_a, y_d, y_out = sem("y_t"), sem("y_a"), sem("y_d"), [sem("y_out0"), sem("y_out1")]

        block = ctx.enter_context(nc.Block())
        w4 = [(0, 2), (2, 4), (4, 6), (6, 8)]
        w4d = [(0, 3), (3, 6), (6, 9), (9, 11)]
        FFN = [(C_FF0, 0), (C_FF1, 1)]

        @block.sync
        def _(sp):
            def slot_free(c):
                if above_zero(c - 1):
                    sp.wait_ge(lo_ok, c - 1)

            def load(w, cols, c, u):
                slot_free(c)
                K_, W_ = w
                view = raw[u][:, 0:K_ * W_].rearrange("p (k n) -> p k n", k=K_)
                for k0, k1 in (w4 if K_ == KD else w4d):
                    sp.dma_start(view[:, k0:k1, :], cols(k0, k1)).then_inc(raw_in[u], 16)

            sp.dma_start(xin[0:META, 0, :], meta_tokens).then_inc(in_x[0], 16)
            sp.dma_start(xin[META:XR, 0, :], x_prompt[0, 0:XR - META, :]).then_inc(in_x[0], 16)
            for t in range(1, 4):
                sp.dma_start(xin[:, t, :], x_prompt[0, XR * t - META:XR * (t + 1) - META, :]).then_inc(in_x[t], 16)
            sp.dma_start(xin[0:NP - 4 * XR, 4, :], x_prompt[0, 4 * XR - META:SEQ, :]).then_inc(in_x[4], 16)
            sp.dma_start(xin[NP - 4 * XR:XR, 4, :], x_sample.rearrange("b t d -> (b t) d")).then_inc(in_x[4], 16)
            sp.dma_start(ident[:], c_ident).then_inc(in_id, 16)

            win = mla_w_in[0].rearrange("(k p) n -> p k n", p=P)
            for c in range(2):
                load((KD, 256), lambda k0, k1: win[:, k0:k1, 256 * c:256 * c + 256], c, c)
            for a, r, n in ((ln_g.rearrange("l s (k p) -> (l s k) p", p=P), V_G, 32),
                            (ln_b.rearrange("l s (k p) -> (l s k) p", p=P), V_B, 32),
                            (lru_conv_w[0].rearrange("j (k p) -> (j k) p", p=P), V_CW, 32)):
                sp.dma_start(prow[r:r + n, 0, :], a).then_inc(in_par, 16)
            for a, r, n in ((lru_conv_b, V_CB, 8), (lru_b_a, V_BA, 8), (lru_b_i, V_BI, 8), (lru_lambda, V_LAM, 8),
                            (mla_q_norm, V_QN, KQ), (mla_kv_norm, V_KN, KC)):
                sp.dma_start(prow[r - 96:r - 96 + n, 1, :],
                             a[0].rearrange("(k p) -> k p", p=P)).then_inc(in_par, 16)
            sp.dma_start(srow[0:24, :], state_conv[0].rearrange("b j d -> (b j) d")).then_inc(in_st, 16)
            sp.dma_start(srow[24:32, :], state_lru_h[0]).then_inc(in_st, 16)
            sp.dma_start(cst[:, 0:P], c_mask).then_inc(in_cst, 16)
            sp.dma_start(cst[:, P:P + B * NS], c_smask).then_inc(in_cst, 16)
            sp.dma_start(trig[:], c_trig).then_inc(in_att, 16)
            sp.dma_start(wuv[:], mla_w_uv[0].rearrange("(k p) h v -> p k (h v)", p=P)).then_inc(in_att, 16)
            sp.dma_start(pages[:], page_table.rearrange("b n -> (b n)").rearrange("(a n) -> a n", a=1)).then_inc(in_pg, 16)
            slot_free(2)
            last = raw[0][:, 0:W_D].rearrange("p (k n) -> p k n", k=KD)
            for d0, s0, n in ((0, 512, 160), (160, 656, 16), (176, 640, 16), (192, 0, 64)):
                sp.dma_start(last[:, :, d0:d0 + n], win[:, :, s0:s0 + n]).then_inc(raw_in[0], 16)
            wo = mla_w_o[0].rearrange("(k p) n -> p k n", p=P)
            for j in range(2):
                load((KD, 256), lambda k0, k1: wo[:, k0:k1, 256 * j:256 * j + 256], C_WO + j, (C_WO + j) % 2)

            wqv = mla_w_q_up[0].rearrange("(k p) n -> p k n", p=P)
            wukv = mla_w_uk[0].rearrange("(k p) h n -> p k (h n)", p=P)
            hw = NOPE + ROPE
            for u in range(2):
                sp.dma_start(wq[u][:, :, 0:hw], wqv[:, :, hw * u:hw * u + hw]).then_inc(wq_in[u], 16)
            sp.dma_start(wuk[:], wukv[:, :, 0:P]).then_inc(wuk_in, 16)

            def sample_pages(b, u, used=None):
                numbers = [sp.value_load(pages[0:1, bass.ds(b * PAGES + n, 1)], min_val=0, max_val=N_POOL - 1)
                           for n in range(PAGES)]
                if used is not None:
                    sp.wait_ge(d_o, used)
                for n, page in enumerate(numbers):
                    sp.dma_start(Ctok[u][:, n:n + 1, 0:KV_R],
                                 cache_latent[0, bass.ds(page, 1)].rearrange("a p c -> p a c")).then_inc(pg_in[u], 16)
                    sp.dma_start(Ctok[u][:, n, KV_R:KV_R + 2 * ROPE].rearrange("p (a c) -> p a c", a=2),
                                 cache_krope[0, bass.ds(page, 1)].rearrange("a p c -> p a c").broadcast_to(
                                     [P, 2, ROPE])).then_inc(pg_in[u], 16)

            sp.wait_ge(s_xt, KD)
            sp.wait_ge(s_pt_, 2)
            sp.wait_ge(s_stt, 1)
            sp.wait_ge(s_cb, 3)
            sp.wait_ge(s_par, 26)
            sp.wait_ge(in_pg, 16)
            for u in range(2):
                sample_pages(u, u)
            with sp.Fori(0, HEADS // 2 - 1) as i:
                for u in range(2):
                    if u == 0:
                        sp.wait_ge(wt_sum, i + 1)
                        sp.dma_start(wuk[:], wukv[:, :, bass.ds(i * P + P, P)]).then_inc(wuk_in, 16)
                    sp.wait_ge(q_sum, i * 2 + (u + 1))
                    sp.dma_start(wq[u][:, :, 0:hw], wqv[:, :, bass.ds(i * (2 * hw) + (u + 2) * hw, hw)]
                                 ).then_inc(wq_in[u], 16)
            sp.wait_ge(sc_sum, HEADS * 5)
            sp.wait_ge(q_rot, HEADS)
            sp.wait_ge(q_dve, HEADS)
            sp.wait_ge(ql_sum, HEADS)
            sp.wait_ge(o_sum, HEADS)
            with sp.Fori(0, 2) as i:
                for s in range(3):
                    sample_pages(i * 3 + (s + 2), (s + 2) % 3, used=i * 3 + s)
            for j in range(2, 4):
                load((KD, 256), lambda k0, k1: wo[:, k0:k1, 256 * j:256 * j + 256], C_WO + j, (C_WO + j) % 2)

            def load_gu(layer, half, c, j, q, u):
                gu = ffn_w_gu[layer].rearrange("(k p) n -> p k n", p=P)
                slot_free(c)
                view = raw[u][:, 0:W_D].rearrange("p (k n) -> p k n", k=KD)
                col = j * P + half * FH * P
                for k0, k1 in ((0, 4), (4, 8)):
                    sp.dma_start(view[:, k0:k1, 0:P], gu[:, k0:k1, bass.ds(col, P)]).then_inc(raw_in[u], 16)
                    sp.dma_start(view[:, k0:k1, P:2 * P], gu[:, k0:k1, bass.ds(col + FF, P)]).then_inc(raw_in[u], 16)

            def ffn(base, layer):
                for half in range(2):
                    b0 = base + 15 * half
                    chunk_loop(sp, b0, FH, lambda c, j, q, u: load_gu(layer, half, c, j, q, u))
                    dn = ffn_w_down[layer].rearrange("(k p) n -> p k n", p=P)[:, half * FH:(half + 1) * FH, :]
                    chunk_loop(sp, b0 + FH, 4, lambda c, j, q, u: load(
                        (FH, 256), lambda k0, k1: dn[:, k0:k1, bass.ds(j * 256, 256)], c, u), tail=0)

            ffn(*FFN[0])

            lin = lru_w_in[0].rearrange("(k p) n -> p k n", p=P)

            def load_lru(c, j, q, u):
                slot_free(c)
                view = raw[u][:, 0:W_D].rearrange("p (k n) -> p k n", k=KD)
                sp.dma_start(view[:, :, 0:P], lin[:, :, bass.ds(j * P, P)]).then_inc(raw_in[u], 16)
                sp.dma_start(view[:, :, P:2 * P], lin[:, :, bass.ds(j * P + D, P)]).then_inc(raw_in[u], 16)
                for n, w in enumerate((lru_w_a, lru_w_i)):
                    sp.dma_start(raw[u][:, W_D + n * P:W_D + n * P + P].rearrange("p (a n) -> p a n", a=1),
                                 w[0, bass.ds(j, 1)].rearrange("a k n -> k a n")).then_inc(raw_in[u], 16)

            chunk_loop(sp, C_LRU, KD, load_lru, tail=0)
            lo_w = lru_w_o[0].rearrange("(k p) n -> p k n", p=P)
            chunk_loop(sp, C_LO, 4, lambda c, j, q, u: load(
                (KD, 256), lambda k0, k1: lo_w[:, k0:k1, bass.ds(j * 256, 256)], c, u), tail=0)
            ffn(*FFN[1])
            for t in range(5):
                sp.wait_ge(y_a, t + 1)
                sp.wait_ge(y_d, t + 1)
                if t < 4:
                    sp.dma_start(y_prompt[0, P * t:P * t + P, :], yrow[t % 2][:]).then_inc(y_out[t % 2], 16)
                else:
                    sp.dma_start(y_sample.rearrange("b t d -> (b t) d"), yrow[0][0:NS, :]).then_inc(y_out[0], 16)
            sp.wait_ge(y_out[0], 48)
            sp.wait_ge(y_out[1], 32)

        @block.tensor
        def _(pe):
            def dense(jp, u, K_, W_, col, rh, rl, done, first=None):
                hi = wh[u][:, 0:K_ * W_].rearrange("p (k n) -> p k n", k=K_)
                lo = wl[u][:, 0:K_ * W_].rearrange("p (k n) -> p k n", k=K_)
                for k in range(K_):
                    if first is not None:
                        first(k)
                    for n, (w, x) in enumerate(((hi, rh), (hi, rl), (lo, rh))):
                        for h in range(2):
                            mm = pe.matmul(ps[:, 1024 * jp + 512 * h:1024 * jp + 512 * h + TH], w[:, k, col:col + P],
                                           x[:, k, h * TH:(h + 1) * TH], start=(k == 0 and n == 0),
                                           stop=(k == K_ - 1 and n == 2))
                mm.then_inc(done, 1)

            def behind_norm(c, u, n, done1):
                pe.wait_ge(lo_ok, c + 1)
                pe.wait_ge(f0_ok, c)
                pe.wait_ge(f1_ok, c)
                hi = wh[u][:, 0:W_D].rearrange("p (k n) -> p k n", k=KD)
                lo = wl[u][:, 0:W_D].rearrange("p (k n) -> p k n", k=KD)
                for k in range(KD):
                    pe.wait_ge(n_lo, KD * n + k + 1)
                    for jp in range(2):
                        for i, (w, x) in enumerate(((hi, xh), (hi, xl), (lo, xh))):
                            for h in range(2):
                                mm = pe.matmul(ps[:, 1024 * jp + 512 * h:1024 * jp + 512 * h + TH],
                                               w[:, k, jp * P:jp * P + P], x[:, k, h * TH:(h + 1) * TH],
                                               start=(k == 0 and i == 0), stop=(k == KD - 1 and i == 2))
                        if k == KD - 1:
                            mm.then_inc((t0_ok, done1)[jp], 1)

            def chunk(c, u, K_, W_, rh, rl, first=None):
                pe.wait_ge(lo_ok, c + 1)
                if above_zero(c):
                    pe.wait_ge(f0_ok, c)
                dense(0, u, K_, W_, 0, rh, rl, t0_ok, first)
                if above_zero(c):
                    pe.wait_ge(f1_ok, c)
                dense(1, u, K_, W_, P, rh, rl, t1_ok)

            def total(bank, n_ones, t, start, stop):
                for h in range(2):
                    mm = pe.matmul(ps[:, bank + 512 * h:bank + 512 * h + TH], ones[:, n_ones, :],
                                   t[:, h * TH:(h + 1) * TH], start=start, stop=stop)
                return mm

            def last_chunks(c, us, K_, rh, rl, n):
                pe.wait_ge(lo_ok, c + 1)
                pe.wait_ge(f0_ok, c)
                dense(0, us[0], K_, 256, 0, rh, rl, t0_ok)
                pe.wait_ge(n_acc, EARLY * n + EARLY - 1)
                total(2048, 3, acc, True, True).then_inc(n_mean, 1)
                pe.wait_ge(f1_ok, c)
                dense(1, us[0], K_, 256, P, rh, rl, t1_ok)
                pe.wait_ge(lo_ok, c + 2)
                pe.wait_ge(f0_ok, c + 1)
                dense(0, us[1], K_, 256, 0, rh, rl, t0_ok)

                def beside(k):
                    if k == K_ - 2:
                        pe.wait_ge(n_acc, EARLY * (n + 1))
                        pe.wait_ge(f0_ok, c + 2)
                        total(0, 0, acc, True, False)
                    if k == K_ - 1:
                        pe.wait_ge(n_dev, KD * n + 7)
                        total(0, 0, xT[:, 6, :], False, False)

                pe.wait_ge(f1_ok, c + 1)
                dense(1, us[1], K_, 256, P, rh, rl, t1_ok, beside)
                pe.wait_ge(n_ssq, 5 * (n + 1))
                total(3072, 0, ssq, True, False)
                pe.wait_ge(n_sq, KD * n + 7)
                total(3072, 0, sq[0], False, False)
                pe.wait_ge(n_dev, KD * n + 8)
                total(0, 0, xT[:, 7, :], False, True).then_inc(n_rest, 1)
                pe.wait_ge(n_sq, KD * n + 8)
                total(3072, 0, sq[1], False, True).then_inc(n_var, 1)
                pe.wait_ge(n_rsq, n + 1)

            pe.wait_ge(in_id, 16)
            for k in range(KD):
                if k >= 4:
                    pe.wait_ge(s_xe, k - 3)
                for t in range(5):
                    if k == 0:
                        pe.wait_ge(in_x[t], 16 if t in (1, 2, 3) else 32)
                    at = 1024 * (k % 4) + (XR * t if t < 3 else 512 + XR * (t - 3))
                    mm = pe.transpose(ps[:, at:at + XR], xin[:, t, k * P:(k + 1) * P], ident[0:XR, 0:XR])
                mm.then_inc(s_xt, 1)
            pe.wait_ge(s_xe, 5)
            pe.wait_ge(in_par, 144)
            pe.transpose(ps[:, 0:96], prow[0:96, 0, :], ident[0:96, 0:96]).then_inc(s_pt_, 1)
            pe.transpose(ps[:, 96:NV], prow[0:NV - 96, 1, :], ident[0:NV - 96, 0:NV - 96]).then_inc(s_pt_, 1)
            pe.wait_ge(s_xe, 6)
            pe.wait_ge(in_st, 32)
            for k in range(KD):
                mm = pe.transpose(ps[:, 1024 + 32 * k:1024 + 32 * k + 32], srow[:, k * P:(k + 1) * P],
                                  ident[0:32, 0:32])
            mm.then_inc(s_stt, 1)

            pe.wait_ge(s_xh0, KD)
            pe.wait_ge(n_lo, KD)
            pe.wait_ge(s_pte, 1)
            pe.wait_ge(s_ste, 1)
            for c in range(3):
                chunk(c, c % 2, KD, 256, xh, xl)
            pe.wait_ge(s_ones, 4)
            for jp, tiles, o in ((2, range(KQ), 1), (3, range(KQ, KQ + KC), 2)):
                for n in tiles:
                    pe.wait_ge(s_zsq, n + 1)
                    for h in range(2):
                        mm = pe.matmul(ps[:, 1024 * jp + 512 * h:1024 * jp + 512 * h + TH], ones[:, o, :],
                                       zsq[:, n, h * TH:(h + 1) * TH], start=(n == tiles[0]), stop=(n == tiles[-1]))
                mm.then_inc(s_zms, 1)
            pe.wait_ge(s_z, KQ + KC)
            pe.wait_ge(s_kr, 4)
            for t in range(6):
                t0, n = (P * t, P) if t < 4 else ((SEQ, META) if t == 4 else (NP, NS))
                if t >= 2:
                    pe.wait_ge(s_lte, t - 1)
                bank = 512 * (t % 2)
                for k in range(KC):
                    pe.transpose(ps[0:n, bank + k * P:bank + (k + 1) * P], z[:, KQ + k, t0:t0 + n], ident[:])
                pe.transpose(ps[0:n, bank + KV_R:bank + KV_R + ROPE], krs[64:96, t0:t0 + n],
                             ident[64:96, 64:96]).then_inc(s_lt, 1)
            pe.wait_ge(in_att, 32)
            g = 0
            for kt in range(5):
                n = P if kt < 4 else META
                for h in range(2):
                    if g >= 6:
                        pe.wait_ge(s_ve if g % 2 == 0 else s_vd, (g - 6) // 2 + 1)
                    bank = 512 * (2 + g % 6)
                    for k in range(KC):
                        mm = pe.matmul(ps[0:n, bank:bank + 512], z[:, KQ + k, kt * P:kt * P + n],
                                       wuv[:, k, h * 512:(h + 1) * 512], start=(k == 0), stop=(k == KC - 1))
                    mm.then_inc(s_v, 1)
                    g += 1

            def keys(p):
                pe.wait_ge(wuk_in, (p + 1) * 16)
                if above_zero(p):
                    pe.wait_ge(o_lo, (p - 1) * 2)
                for h in range(2):
                    for k in range(KC):
                        mm = pe.matmul(ps[:, 512 * (6 + h):512 * (6 + h) + NP // 2], wuk[:, k, :],
                                       z[:, KQ + k, h * (NP // 2):(h + 1) * (NP // 2)], start=(k == 0), stop=(k == KC - 1))
                mm.then_inc(k_sum, 1)

            def queries(h, u, n):
                if n == 0:
                    pe.wait_ge(wq_sw, h * 2 + 2)
                for k in range(KQ):
                    mm = pe.matmul(ps[:, 512 * n:512 * n + TH], wq[u][:, k, :], z[:, k, n * TH:(n + 1) * TH],
                                   start=(k == 0), stop=(k == KQ - 1))
                if n == 1:
                    mm.then_inc(q_sum, 1)

            def scores(h, u, i):
                n = P if i < 4 else META
                bank = 512 * (2 + i % 2)
                if above_zero(h * 5 + (0, 0, 1, 2, 4)[i]):
                    pe.wait_ge(sc_exp, h * 5 + (0, 0, 1, 2, 4)[i])
                w = P * i + n
                q = Q[u][:, P * i:P * i + n]
                if i < 4:
                    pe.matmul(ps[0:n, bank:bank + w], q, K[u][:, 0:w], start=True, stop=False)
                    mm = pe.matmul(ps[0:n, bank + P * i:bank + w], identb[:], maskb[:], start=False, stop=True)
                else:
                    pe.matmul(ps[0:n, 1024:1536], q, K[u][:, 0:512], start=True, stop=True)
                    pe.matmul(ps[0:n, 1536:1536 + n], q, K[u][:, 512:NP], start=True, stop=False)
                    mm = pe.matmul(ps[0:n, 1536:1536 + n], identb[0:n, 0:n], maskb[0:n, 0:n], start=False, stop=True)
                mm.then_inc(sc_sum, 1)

            def turn(h, u, i):
                n = P if i < 4 else META
                pe.wait_ge(sc_nrm, h * 5 + (i + 1))
                if above_zero(h * 6 + max(0, i - 1)):
                    pe.wait_ge(pt_rd, h * 6 + max(0, i - 1))
                bank = 512 * (4 + i % 2)
                for j in range(i + 1):
                    kk = P if j < 4 else META
                    m = P if j == 0 else n
                    at = PR_AT[i] + j * P
                    mm = pe.transpose(ps[0:kk, bank + j * n:bank + j * n + m], Pr[u][0:m, at:at + kk],
                                      ident[0:m, 0:m])
                mm.then_inc(pt_sum, 1)

            def outputs(h, u):
                pe.wait_ge(pt_rd, h * 6 + 6)
                pe.wait_ge(v_cp, h * 2 + 2)
                if above_zero(h):
                    pe.wait_ge(o_lo, h)
                hp = NP // 2
                for j in range(5):
                    kk = P if j < 4 else META
                    for half in range(2):
                        q0 = max(P * j, half * hp)
                        q1 = (half + 1) * hp
                        if q0 >= q1:
                            continue
                        at = 512 * (6 + half) + q0 - half * hp
                        mm = pe.matmul(ps[64 * u:64 * u + VH, at:at + q1 - q0], Vs[u][0:kk, j, :],
                                       PT[:, j, q0:q1] if j < 4 else PT4[:],
                                       start=(j == 0), stop=(j == 4 or (half == 0 and j == 2)))
                mm.then_inc(o_sum, 1)

            def head(p, u, first=False):
                h, v = p * 2 + u, 1 - u
                last = isinstance(h, int) and h == HEADS - 1
                if u == 0:
                    pe.wait_ge(k_act, p + 1)
                    pe.wait_ge(k_dve, p + 1)
                pe.wait_ge(q_act, h + 1)
                pe.wait_ge(q_dve, h + 1)
                for i in range(5):
                    scores(h, u, i)
                    if not first:
                        turn(h - 1, v, i)
                    if i == 0 and u == 0:
                        for k in range(KC):
                            mm = pe.transpose(ps[:, k * P:(k + 1) * P], wuk[:, k, :], ident[:])
                        mm.then_inc(wt_sum, 1)
                    if i == 1 and u == 1 and not last:
                        keys(p + 1)
                    if i == 2:
                        pe.wait_ge(wt_rd, p + 1)
                        for k in range(KC):
                            mm = pe.matmul(ps[:, 512 + NS * k:512 + NS * (k + 1)], wukT[u][:, k * P:(k + 1) * P],
                                           Q[u][0:NOPE, NP:T], start=True, stop=True)
                        mm.then_inc(ql_sum, 1)
                    if i == 3 and not last:
                        queries(h + 1, v, 0)
                if not last:
                    pe.wait_ge(ql_rd, h + 1)
                    queries(h + 1, v, 1)
                if not first:
                    if u == 1 and not last:
                        pe.wait_ge(k_act, p + 2)
                        pe.wait_ge(k_dve, p + 2)
                    outputs(h - 1, v)

            pe.wait_ge(s_lte, 6)
            for n in range(2):
                queries(0, 0, n)
            pe.wait_ge(s_ve, 5)
            pe.wait_ge(s_vd, 5)
            keys(0)
            pe.wait_ge(s_kp2, 2)
            pe.wait_ge(s_cb, 3)
            head(0, 0, True)
            with pe.Fori(0, HEADS // 2 - 1) as i:
                head(i, 1)
                head(i + 1, 0)
            head(HEADS // 2 - 1, 1)
            for i in range(5):
                turn(HEADS - 1, 1, i)
            outputs(HEADS - 1, 1)

            def fill(n, u, f):
                at = (0, 2, 4, 1, 3, 5).index(f)
                by, count = ((d_fd, -1), (d_fd, 0), (d_fa, 1), (d_fa, 2), (d_fa, 3), (d_fd, 1))[at]
                if above_zero(n * 3 + count):
                    pe.wait_ge(by, n * 3 + count)
                bank = 512 * (4 + at % 2)
                for k in range(4):
                    pg = 4 * (f % 2) + k
                    if f < 4:
                        mm = pe.transpose(ps[:, bank + k * P:bank + (k + 1) * P],
                                          Ctok[u][:, pg, (f // 2) * P:(f // 2 + 1) * P], ident[:])
                    else:
                        mm = pe.transpose(ps[:, bank + k * P:bank + (k + 1) * P],
                                          Ctok[u][:, pg, KV_R - 64:KV_R + 64], ident[:])
                mm.then_inc(d_fill, 1)

            def sample_scores(b, u, kb):
                out = ps[0:ROWS, 512 * kb:512 * kb + (512 if kb < 2 else NS)]
                for k in range(KC):
                    rhs = CT[:, k, 512 * kb:512 * kb + 512] if kb < 2 else z[:, KQ + k, NP:T]
                    pe.matmul(out, qs[u][:, k, :], rhs, start=(k == 0), stop=False)
                rhs = CTR[64:P, 512 * kb:512 * kb + 512] if kb < 2 else krs[64:P, NP:T]
                mm = pe.matmul(out, qrs[u][64:P, :], rhs, start=False, stop=(kb < 2))
                if kb == 2:
                    pe.matmul(out, identb[:, 0:ROWS],
                              smaskb[:, b, :] if isinstance(b, int) else smaskb[:, bass.ds(b, 1), :],
                              start=False, stop=True)
                return mm

            def sample_turn(b):
                pe.wait_ge(d_nrm, b + 1)
                if above_zero(b):
                    pe.wait_ge(d_od, b)
                for k in range(PAGES):
                    m = P if k == 0 else ROWS
                    pe.transpose(ps[:, 3072 + ROWS * k:3072 + ROWS * k + m], Ps[0:m, k * P:(k + 1) * P],
                                 ident[0:m, 0:m])
                pe.transpose(ps[0:NS, 3584:3584 + ROWS], Ps[0:ROWS, PAST:PAST + NS], ident[0:ROWS, 0:ROWS]).then_inc(d_pt, 1)

            def sample_out(b, u):
                pe.wait_ge(d_pa, b + 1)
                pe.wait_ge(d_pd, b + 1)
                if above_zero(b):
                    pe.wait_ge(d_oa, b)
                for k in range(KC):
                    at = (1536, 3712)[k]
                    out = ps[:, at:at + ROWS]
                    for j in range(PAGES):
                        pe.matmul(out, Ctok[u][:, j, k * P:(k + 1) * P], PTs[:, j, :], start=(j == 0), stop=False)
                    mm = pe.matmul(out, cnew[:, k * P:(k + 1) * P], PTn[:], start=False, stop=True)
                mm.then_inc(d_o, 1)

            def sample(b, u, rounds, more=True):
                first = isinstance(b, int) and b == 0
                nu, pu = (u + 1) % 3, (u - 1) % 3
                pe.wait_ge(d_fa, b * 3 + 3)
                pe.wait_ge(d_q, b * 2 + 2)
                if not first:
                    pe.wait_ge(d_exp, b)
                sample_scores(b, u, 0)
                if not first:
                    sample_turn(b - 1)
                sample_scores(b, u, 2)
                if not first:
                    sample_out(b - 1, pu)
                pe.wait_ge(d_fd, b * 3 + 3)
                sample_scores(b, u, 1).then_inc(d_s, 1)
                if more:
                    pe.wait_ge(pg_in[nu], rounds * 256)
                    for f in (0, 2, 4, 1, 3, 5):
                        fill(b + 1, nu, f)

            pe.wait_ge(o_lo, HEADS)
            pe.wait_ge(pg_in[0], 256)
            for f in (0, 2, 4, 1, 3, 5):
                fill(0, 0, f)
            sample(0, 0, 1)
            with pe.Fori(0, 2) as i:
                for s in range(3):
                    sample(i * 3 + (s + 1), (s + 1) % 3, i + (s + 5) // 3)
            sample(B - 1, (B - 1) % 3, 0, False)
            sample_turn(B - 1)
            sample_out(B - 1, (B - 1) % 3)
            pe.wait_ge(d_oa, B)
            pe.wait_ge(d_od, B)
            for h in range(HEADS):
                for k in range(KC):
                    mm = pe.matmul(ps[64 * (h % 2):64 * (h % 2) + VH, NS * (h // 2):NS * (h // 2 + 1)],
                                   wuv[:, k, VH * h:VH * (h + 1)], OL[:, k, h, :, :].rearrange("p b t -> p (b t)"),
                                   start=(k == 0), stop=(k == KC - 1))
            mm.then_inc(d_v, 1)

            pe.wait_ge(d_vl, 1)
            for c in (C_WO, C_WO + 1):
                chunk(c, c % 2, KD, 256, xh, xl)
            last_chunks(C_WO + 2, (C_WO % 2, 1 - C_WO % 2), KD, xh, xl, 0)

            def ffn(base, layer, n):
                for half in range(2):
                    b0 = base + 15 * half
                    if half == 0:
                        behind_norm(b0, b0 % 2, n + 1, t1_ok)
                    chunk_loop(pe, b0 + (half == 0), FH - (half == 0),
                               lambda c, j, q, u: chunk(c, u, KD, 256, xh, xl), tail=0)
                    pe.wait_ge(m_l, (layer * 2 + half + 1) * FH)
                    body = lambda c, j, q, u: chunk(c, u, FH, 256, hh, hl)
                    if half == 0:
                        chunk_loop(pe, b0 + FH, 4, body, tail=0)
                    else:
                        c = b0 + FH
                        for j in range(2):
                            chunk(c + j, (c + j) % 2, FH, 256, hh, hl)
                        last_chunks(c + 2, (c % 2, 1 - c % 2), FH, hh, hl, n + 1)

            ffn(C_FF0, 0, 0)

            def lru(c, j, q, u):
                if isinstance(c, int) and c == C_LRU:
                    behind_norm(c, u, 2, r_g)
                else:
                    pe.wait_ge(lo_ok, c + 1)
                    pe.wait_ge(f0_ok, c)
                    dense(0, u, KD, 256, 0, xh, xl, t0_ok)
                    pe.wait_ge(f1_ok, c)
                    dense(1, u, KD, 256, P, xh, xl, r_g)
                pe.wait_ge(r_xl, j + 1)
                pe.wait_ge(r_ge, j * 2)
                for g in range(2):
                    for n, (w, x) in enumerate(((wh[u], xch), (wh[u], xcl), (wl[u], xch))):
                        for h in range(2):
                            at = 1024 * (2 + g) + 512 * h
                            mm = pe.matmul(ps[:, at:at + TH], w[:, W_D + g * P:W_D + (g + 1) * P],
                                           x[:, h * TH:(h + 1) * TH], start=(n == 0), stop=(n == 2))
                mm.then_inc(t1_ok, 1)

            chunk_loop(pe, C_LRU, KD, lru, head=1)
            pe.wait_ge(r_hc, KD)
            pe.wait_ge(r_hh, KD)
            pe.wait_ge(r_ge, 2 * KD)
            for k in range(KD):
                mm = pe.transpose(ps[0:36, 2048 + k * P:2048 + (k + 1) * P], hist[:, k, :], ident[:])
            mm.then_inc(r_t, 1)
            pe.wait_ge(r_yl, KD)
            for c in (C_LO, C_LO + 1):
                chunk(c, c % 2, KD, 256, yh, yl)
            pe.wait_ge(r_te, 2)
            last_chunks(C_LO + 2, (C_LO % 2, 1 - C_LO % 2), KD, yh, yl, 2)
            ffn(C_FF1, 1, 2)
            for t in range(5):
                n = P if t < 4 else NS
                t0 = META + P * t
                if t == 0:
                    pe.wait_ge(n_hi, KD * 4)
                if t >= 2:
                    pe.wait_ge(y_a, t - 1)
                    pe.wait_ge(y_d, t - 1)
                for k in range(KD):
                    at = 1024 * (t % 2) + k * P
                    mm = pe.transpose(ps[0:n, at:at + P], xT[:, k, t0:t0 + n], ident[:])
                mm.then_inc(y_t, 1)

        @block.scalar
        def _(act):
            def split(c, q, u, w):
                act.wait_ge(raw_in[u], q * 64 + 64)
                if above_zero(c - 1):
                    act.wait_ge(t1_ok, c - 1)
                act.activation(wh[u][:, 0:w], raw[u][:, 0:w], ACT.Copy).then_inc(hi_ok, 1)

            def split_next(c, q, u, w):
                if isinstance(c, int):
                    split(c + 1, (c + 1) // 2, (c + 1) % 2, chunk_cols(c + 1))
                else:
                    split(c + 1, q + u, 1 - u, w)

            for k in range(KD):
                act.wait_ge(s_xe, k + 1)
                act.activation(xh[:, k, :], xT[:, k, :], ACT.Copy).then_inc(s_xh0, 1)
            split(0, 0, 0, W_D)
            act.wait_ge(s_par, 2)
            act.activation(spt[:, 1, :], spt[:, 0, :], ACT.Exp).then_inc(s_parA, 1)
            for c in range(3):
                if c < 2:
                    split_next(c, 0, 0, 0)
                act.wait_ge(t0_ok, c + 1)
                act.activation(halves(z[:, 2 * c, :]), pair(0), ACT.Copy).then_inc(f0_ok, 1)
            act.wait_ge(t1_ok, 3)
            for n in range(KQ + KC):
                act.wait_ge(f0_ok, n // 2 + 1)
                if n % 2:
                    act.wait_ge(f1_ok, n // 2 + 1)
                act.activation(zsq[:, n, :], z[:, n, :], ACT.Square).then_inc(s_zsq, 1)
            for n in range(2):
                act.wait_ge(s_zeps, n + 1)
                act.activation(stat[:, n, :], stat[:, n, :], ACT.Sqrt).then_inc(s_zroot, 1)
            for t in range(6):
                n = P if t < 4 else (META if t == 4 else NS)
                act.wait_ge(s_lt, t + 1)
                if t in (2, 3, 4):
                    act.wait_ge(s_lout[t % 2], 32 * (t // 2))
                dst = lat[t % 2] if t < 5 else cnew
                act.activation(dst[0:n, :], ps[0:n, 512 * (t % 2):512 * (t % 2) + KV_R + ROPE],
                               ACT.Copy).then_inc(s_lte, 1)
            for g in range(0, 10, 2):
                kt, h = g // 2, g % 2
                n = P if kt < 4 else META
                act.wait_ge(s_v, g + 1)
                bank = 512 * (2 + g % 6)
                act.activation(V[0:n, kt, h * 512:(h + 1) * 512], ps[0:n, bank:bank + 512], ACT.Copy).then_inc(s_ve, 1)

            def exp(h, u, i):
                n = P if i < 4 else META
                w = P * i + n
                act.wait_ge(sc_max, h * 5 + (i + 1))
                act.activation(Pr[u][0:n, PR_AT[i]:PR_AT[i] + w], ps[0:n, 512 * (2 + i % 2):512 * (2 + i % 2) + w],
                               ACT.Exp, bias=mx[0:n, i % 2:i % 2 + 1],
                               accum_out=rsum[0:n, i % 2:i % 2 + 1]).then_inc(sc_exp, 1)

            def read_pt(h, i):
                n = P if i < 4 else META
                m = min(i + 1, 4)
                bank = 512 * (4 + i % 2)
                act.wait_ge(pt_sum, h * 5 + (i + 1))
                act.activation(PT[:, 0:m, P * i:P * i + n],
                               ps[:, bank:bank + m * n].rearrange("p (j q) -> p j q", j=m), ACT.Copy).then_inc(pt_rd, 1)
                if i == 4:
                    act.activation(PT4[:], ps[0:META, bank + 4 * n:bank + 5 * n], ACT.Copy).then_inc(pt_rd, 1)

            def read_k(p):
                act.wait_ge(k_sum, p + 1)
                act.activation(K[0][0:NOPE, :].rearrange("p (h c) -> p h c", h=2), pair(3, 0, 64)[:, :, 0:NP // 2],
                               ACT.Copy).then_inc(k_act, 1)

            def read_q(h, u):
                act.wait_ge(q_sum, h + 1)
                if above_zero(h - 1):
                    act.wait_ge(q_rot, h - 1)
                act.activation(halves(Q[u][0:NOPE, :]), pair(0, 0, 64), ACT.Copy, scale=SCALE).then_inc(q_act, 1)

            def outputs_hi(h, p, u):
                act.wait_ge(o_sum, h + 1)
                dst = xh[64 * u:64 * u + 64, bass.ds(p, 1), 0:NP].rearrange("p a (h c) -> p (a h) c", h=2)
                act.activation(dst, pair(3, 64 * u, 64 * u + 64)[:, :, 0:NP // 2], ACT.Copy).then_inc(o_hi, 1)

            def head(p, u, first=False):
                h, v = p * 2 + u, 1 - u
                last = isinstance(h, int) and h == HEADS - 1
                for i in range(5):
                    exp(h, u, i)
                    if i == 4 and u == 1 and not last:
                        act.wait_ge(sc_sum, h * 5 + 5)
                        read_k(p + 1)
                    if not first:
                        read_pt(h - 1, i)
                    if i == 0 and u == 0:
                        act.wait_ge(wt_sum, p + 1)
                        for s in range(2):
                            ins = act.activation(wukT[s][:], ps[64 * s:64 * s + 64, 0:KV_R], ACT.Copy)
                        ins.then_inc(wt_rd, 1)
                if not last:
                    read_q(h + 1, v)
                if not first:
                    outputs_hi(h - 1, p + (u - 1), v)

            read_q(0, 0)
            read_k(0)
            head(0, 0, True)
            with act.Fori(0, HEADS // 2 - 1) as i:
                head(i, 1)
                head(i + 1, 0)
            head(HEADS // 2 - 1, 1)
            for i in range(5):
                read_pt(HEADS - 1, i)
            outputs_hi(HEADS - 1, HEADS // 2 - 1, 1)

            def fills(n, parts):
                for at in parts:
                    f = {0: 0, 1: 2, 2: 4}[at]
                    act.wait_ge(d_fill, n * 6 + (at + 1))
                    half = slice(512 * (f % 2), 512 * (f % 2) + 512)
                    dst = CT[:, f // 2, half] if f < 4 else CTR[64:P, half]
                    bank = 512 * (4 + at % 2)
                    act.activation(dst, ps[P - dst.shape[0]:P, bank:bank + 512], ACT.Copy).then_inc(d_fa, 1)

            def turned(b):
                act.wait_ge(d_pt, b + 1)
                act.activation(PTs[:].rearrange("p j r -> p (j r)"), ps[:, 3072:3584], ACT.Copy).then_inc(d_pa, 1)

            def latent_out(b):
                act.wait_ge(d_o, b + 1)
                act.activation(OL[:, 0, :, bass.ds(b, 1), :].rearrange("p h a t -> p h (a t)"),
                               ps[:, 1536:1536 + ROWS].rearrange("p (h t) -> p h t", t=TS), ACT.Copy).then_inc(d_oa, 1)

            def sample(b, more=True):
                first = isinstance(b, int) and b == 0
                if not first:
                    turned(b - 1)
                    latent_out(b - 1)
                if more:
                    fills(b + 1, (0, 1, 2))
                act.wait_ge(d_max, b + 1)
                act.activation(Ps[0:ROWS, :], ps[0:ROWS, 0:PAST + NS], ACT.Exp, bias=mx[0:ROWS, 0:1],
                               accum_out=rsum[0:ROWS, 0:1]).then_inc(d_exp, 1)

            fills(0, (0, 1, 2))
            sample(0)
            with act.Fori(0, 2) as i:
                for s in range(3):
                    sample(i * 3 + (s + 1))
            split(C_WO, C_WO // 2, C_WO % 2, W_D)
            sample(B - 1, False)
            turned(B - 1)
            latent_out(B - 1)
            act.wait_ge(d_v, 1)
            act.activation(xh[:, :, NP:T], ps[:, 0:KD * NS].rearrange("p (k t) -> p k t", k=KD), ACT.Copy).then_inc(d_vh, 1)
            def square(n, k):
                act.wait_ge(n_dev, KD * n + k + 1)
                if k >= 3:
                    act.wait_ge(n_ssq, 5 * n + k - 2)
                act.activation((sq[k % 2] if k else ssq)[:], xT[:, k, :], ACT.Square).then_inc(n_sq, 1)

            def splits_norm(c, n):
                for j in range(3):
                    split_next(c + j, 0, 0, 0)
                for k in range(5):
                    square(n, k)
                if c + 4 < C_END:
                    split_next(c + 3, 0, 0, 0)
                for k in range(5, KD):
                    square(n, k)
                    if k == KD - 2:
                        act.activation(spare[:], ones[:, 0, 0:1], ACT.Sqrt)

            splits_norm(C_WO, 0)

            def norm(n, final=False):
                act.wait_ge(n_rest, n + 1)
                act.activation(halves(acc[:]), pair(0), ACT.Copy).then_inc(n_rcp, 1)
                act.activation(halves(stat[:, 1, :]), pair(0), ACT.Square).then_inc(n_rsq, 1)
                act.wait_ge(n_eps, n + 1)
                act.activation(stat[:, 1, :], stat[:, 0, :], ACT.Sqrt).then_inc(n_root, 1)
                for k in range(KD):
                    act.wait_ge(n_t, KD * n + k + 1)
                    bias = vec[:, V_B + KD * n + k:V_B + KD * n + k + 1]
                    dst = xT if final else xh
                    act.activation(dst[:, k, :], xT[:, k, :], ACT.Identity, bias=bias).then_inc(n_hi, 1)

            def up(base, layer, half, c, j, q, u):
                split_next(c, q, u, W_D)
                act.wait_ge(t0_ok, c + 1)
                act.activation(halves(sg[u][:]), pair(0), ACT.Silu).then_inc(f0_ok, 1)
                act.wait_ge(f1_ok, c + 1)
                act.activation(hh[:, bass.ds(j, 1), :].rearrange("p a t -> p (a t)"), ht[u][:], ACT.Copy).then_inc(m_h, 1)

            def ffn(base, layer):
                for half in range(2):
                    b0 = base + 15 * half
                    chunk_loop(act, b0, FH, lambda c, j, q, u: up(b0, layer, half, c, j, q, u))
                    if half == 0:
                        for c in range(b0 + FH, b0 + 15):
                            split_next(c, 0, 0, 0)
                splits_norm(base + 26, 2 * layer + 1)

            norm(0)
            ffn(*FFN[0])
            norm(1)

            def col(t, n, j):
                return t[:, bass.ds(j + n, 1)]

            def gates(c, j, u):
                act.wait_ge(t1_ok, c + 1)
                for g in range(2):
                    act.activation(halves(gr[u][:, g, :]), pair(2 + g), ACT.Tanh, scale=0.5,
                                   bias=col(hvec, KD * g, j)).then_inc(r_ge, 1)
                act.wait_ge(r_ge, j * 2 + 1)
                act.activation(av[u][:], gr[u][:, 0, :], ACT.Exp, scale=cdec[:, 0, bass.ds(j, 1)],
                               bias=cdec[:, 0, bass.ds(j, 1)]).then_inc(r_a, 1)
                act.activation(th[u][:], gr[u][:, 0, :], ACT.Tanh, scale=cdec[:, 1, bass.ds(j, 1)],
                               bias=cdec[:, 1, bass.ds(j, 1)]).then_inc(r_th, 1)

            def scale_of_input(j, u):
                act.wait_ge(r_v, j + 1)
                act.activation(th[u][:], th[u][:], ACT.Sqrt, scale=0.25).then_inc(r_sq, 1)

            def lru(c, j, q, u):
                if above_zero(j):
                    gates(c - 1, j - 1, 1 - u)
                split_next(c, q, u, W_LRU)
                act.wait_ge(t0_ok, c + 1)
                if above_zero(j - 1):
                    act.wait_ge(r_cv, j * 3 - 3)
                    act.wait_ge(r_hc, j - 1)
                act.activation(U[u][:, 3:3 + TH], ps[:, 0:TH], ACT.Copy)
                act.activation(U[u][:, 3 + TH:UP], ps[:, 512:512 + NP - TH], ACT.Copy)
                act.activation(U[u][:, UP:UL].rearrange("p (b s) -> p b s", b=B)[:, :, 3:7],
                               ps[:, 512 + NP - TH:512 + TH].rearrange("p (b s) -> p b s", b=B),
                               ACT.Copy).then_inc(f0_ok, 1)
                act.wait_ge(f0_ok, c + 1)
                act.wait_ge(r_pad, j + 1)
                if above_zero(j):
                    act.wait_ge(r_ix, j * 2)
                act.activation(xc[:, 0:UL - 3], U[u][:, 0:UL - 3], ACT.Identity, scale=col(vec, V_CW, j),
                               bias=col(vec, V_CB, j)).then_inc(r_x0, 1)
                if above_zero(j):
                    scale_of_input(j - 1, 1 - u)
                act.wait_ge(r_cv, j * 3 + 3)
                act.wait_ge(t1_ok, c)
                act.activation(xch[:, 0:NP], xc[:, 0:NP], ACT.Copy)
                act.activation(xch[:, NP:T].rearrange("p (b s) -> p b s", b=B),
                               samples_of(xc), ACT.Copy).then_inc(r_xh, 1)
                act.wait_ge(r_g, j + 1)
                if above_zero(j - 1):
                    act.wait_ge(r_yl, j - 1)
                act.activation(halves(gel[u][:]), pair(1), ACT.Gelu_apprx_tanh).then_inc(f1_ok, 1)

            chunk_loop(act, C_LRU, KD, lru, head=2)
            gates(C_LRU + KD - 1, KD - 1, (KD - 1 + C_LRU) % 2)
            scale_of_input(KD - 1, (KD - 1 + C_LRU) % 2)
            act.wait_ge(r_t, 1)
            act.activation(hrow[:, 0:512], ps[0:36, 2048:2560], ACT.Copy).then_inc(r_te, 1)
            splits_norm(C_LO, 2)
            norm(2)
            ffn(*FFN[1])
            norm(3, True)
            for t in range(5):
                n = P if t < 4 else NS
                act.wait_ge(y_t, t + 1)
                if t >= 2:
                    act.wait_ge(y_out[t % 2], 16 * (t // 2))
                act.activation(yrow[t % 2][0:n, 0:512], ps[0:n, 1024 * (t % 2):1024 * (t % 2) + 512],
                               ACT.Copy).then_inc(y_a, 1)

        @block.vector
        def _(dve):
            def split(c, u, w):
                dve.wait_ge(hi_ok, c + 1)
                dve.tensor_tensor(wl[u][:, 0:w], raw[u][:, 0:w], wh[u][:, 0:w].bitcast(F32),
                                  ALU.subtract).then_inc(lo_ok, 1)

            def split_next(c, u, w):
                if isinstance(c, int):
                    split(c + 1, (c + 1) % 2, chunk_cols(c + 1))
                else:
                    split(c + 1, 1 - u, w)

            for n, v in enumerate((1.0 / D, 1.0 / QL_R, 1.0 / KV_R, 1.0 / (EARLY * P))):
                dve.memset(ones[:, n, :], v).then_inc(s_ones, 1)
            for k in range(KD + 1):
                if k < KD:
                    dve.wait_ge(s_xt, k + 1)
                    at = 1024 * (k % 4)
                    dve.tensor_copy(xT[:, k, 0:3 * XR], ps[:, at:at + 3 * XR])
                    dve.tensor_copy(xT[:, k, 3 * XR:T], ps[:, at + 512:at + 512 + 2 * XR]).then_inc(s_xe, 1)
                if k >= 1:
                    dve.wait_ge(s_xh0, k)
                    dve.tensor_tensor(xl[:, k - 1, :], xT[:, k - 1, :], xh[:, k - 1, :].bitcast(F32),
                                      ALU.subtract).then_inc(n_lo, 1)
            split(0, 0, W_D)
            dve.wait_ge(s_pt_, 2)
            dve.tensor_copy(vec[:], ps[:, 0:NV]).then_inc(s_pte, 1)
            dve.wait_ge(s_stt, 1)
            dve.tensor_copy(stT[:].rearrange("p k r -> p (k r)"), ps[:, 1024:1024 + 32 * KD]).then_inc(s_ste, 1)
            steps = [0]

            def step(ins):
                steps[0] += 1
                ins.then_inc(s_par, 1)
                dve.wait_ge(s_par, steps[0])

            lam = vec[:, V_LAM:V_LAM + KD]
            neg, y, s2, ser, den, sv = (spt[:, n, :] for n in range(6))
            dve.wait_ge(s_pte, 1)
            step(dve.tensor_scalar(s2, lam, -1.0, None, ALU.mult))
            step(dve.tensor_tensor(neg, lam, s2, ALU.min))
            split_next(0, 0, 0)
            dve.wait_ge(s_parA, 1)
            step(dve.tensor_scalar(den, y, 2.0, None, ALU.add))
            step(dve.reciprocal(sv, den))
            step(dve.tensor_tensor(sv, sv, y, ALU.mult))
            step(dve.tensor_tensor(s2, sv, sv, ALU.mult))
            step(dve.tensor_scalar(ser, s2, 1.0 / 17, 1.0 / 15, ALU.mult, ALU.add))
            for d in (13, 11, 9, 7, 5, 3, 1):
                step(dve.tensor_tensor(ser, ser, s2, ALU.mult))
                step(dve.tensor_scalar(ser, ser, 1.0 / d, None, ALU.add))
            step(dve.tensor_tensor(ser, ser, sv, ALU.mult))
            step(dve.tensor_scalar(s2, lam, -1.0, 0.0, ALU.mult, ALU.max))
            step(dve.scalar_tensor_tensor(s2, ser, 2.0, s2, ALU.mult, ALU.add))
            step(dve.tensor_scalar(cdec[:, 0, :], s2, -LRU_C / 2, None, ALU.mult))
            step(dve.tensor_scalar(cdec[:, 1, :], s2, LRU_C / 2, None, ALU.mult))
            dve.tensor_scalar(hvec[:], vec[:, V_BA:V_BA + 16], 0.5, None, ALU.mult).then_inc(s_par, 1)

            for c in range(3):
                if c == 1:
                    split_next(1, 0, 0)
                dve.wait_ge(t1_ok, c + 1)
                if c < 2:
                    dve.tensor_copy(halves(z[:, 2 * c + 1, :]), pair(1)).then_inc(f1_ok, 1)
            dve.wait_ge(in_att, 32)
            dve.tensor_tensor(halves(rt[:, 0, :]), pair(1, 0, 32), halves(trig[0:32, :]), ALU.mult).then_inc(s_kr, 1)
            dve.tensor_tensor(halves(rt[:, 1, :]), pair(1, 32, 64), halves(trig[32:64, :]), ALU.mult).then_inc(f1_ok, 1)
            dve.wait_ge(f1_ok, 3)
            dve.wait_ge(s_kr, 1)
            for r in (64, 96):
                dve.tensor_tensor(krs[r:r + 32, :], rt[:, 0, :], rt[:, 1, :], ALU.add).then_inc(s_kr, 1)
            for n in range(2):
                dve.wait_ge(s_zms, n + 1)
                dve.tensor_scalar(halves(stat[:, n, :]), pair(2 + n), EPS, None, ALU.add).then_inc(s_zeps, 1)
            for n in range(2):
                dve.wait_ge(s_zroot, n + 1)
                dve.reciprocal(stat[:, n, :], stat[:, n, :]).then_inc(s_zinv, 1)
            for n in range(KQ + KC):
                dve.wait_ge(s_zinv, 1 if n < KQ else 2)
                g = V_QN + n
                dve.scalar_tensor_tensor(z[:, n, :], z[:, n, :], vec[:, g:g + 1], stat[:, 0 if n < KQ else 1, :],
                                         ALU.mult, ALU.mult).then_inc(s_z, 1)
            dve.nop().then_inc(s_kr, 1)
            for g in range(1, 10, 2):
                kt, h = g // 2, g % 2
                n = P if kt < 4 else META
                dve.wait_ge(s_v, g + 1)
                bank = 512 * (2 + g % 6)
                dve.tensor_copy(V[0:n, kt, h * 512:(h + 1) * 512], ps[0:n, bank:bank + 512]).then_inc(s_vd, 1)

            def top_score(h, i):
                n = P if i < 4 else META
                w = P * i + n
                dve.wait_ge(sc_sum, h * 5 + (i + 1))
                dve.tensor_reduce(mx[0:n, i % 2:i % 2 + 1], ps[0:n, 512 * (2 + i % 2):512 * (2 + i % 2) + w], AX.X,
                                  ALU.max, negate=True).then_inc(sc_max, 1)

            def normalise(h, u, i):
                n = P if i < 4 else META
                w = P * i + n
                dve.wait_ge(sc_exp, h * 5 + (i + 1))
                dve.reciprocal(rsum[0:n, 2 + i % 2:3 + i % 2], rsum[0:n, i % 2:i % 2 + 1]).then_inc(sc_inv, 1)
                dve.wait_ge(sc_inv, h * 5 + (i + 1))
                p = Pr[u][0:n, PR_AT[i]:PR_AT[i] + w]
                dve.tensor_scalar(p, p, rsum[0:n, 2 + i % 2:3 + i % 2], None, ALU.mult).then_inc(sc_nrm, 1)

            def read_k(p):
                dve.wait_ge(k_sum, p + 1)
                dve.tensor_copy(K[1][0:NOPE, :].rearrange("p (h c) -> p h c", h=2),
                                pair(3, 64, P)[:, :, 0:NP // 2]).then_inc(k_dve, 1)

            def read_q(h, u):
                dve.wait_ge(q_sum, h + 1)
                if above_zero(h - 1):
                    dve.wait_ge(q_rot, h - 1)
                dve.tensor_tensor(halves(Q[u][64:P, :]), pair(0, 64, P), halves(trig[64:P, :]), ALU.mult).then_inc(q_dve, 1)

            def outputs_lo(h, p, u):
                dve.wait_ge(o_hi, h + 1)
                rows = slice(64 * u, 64 * u + 64)
                dst = xl[rows, bass.ds(p, 1), 0:NP].rearrange("p a (h c) -> p (a h) c", h=2)
                hi = xh[rows, bass.ds(p, 1), 0:NP].rearrange("p a (h c) -> p (a h) c", h=2)
                dve.tensor_tensor(dst, pair(3, 64 * u, 64 * u + 64)[:, :, 0:NP // 2], hi.bitcast(F32),
                                  ALU.subtract).then_inc(o_lo, 1)

            def head(p, u, first=False):
                h, v = p * 2 + u, 1 - u
                last = isinstance(h, int) and h == HEADS - 1
                for i in range(5):
                    top_score(h, i)
                    if i >= 1:
                        normalise(h, u, i - 1)
                    if i == 2:
                        dve.wait_ge(ql_sum, h + 1)
                        for k in range(KC):
                            dst = qlat[:, k, :, bass.ds(h, 1), :].rearrange("p b a t -> p b (a t)")
                            src = ps[:, 512 + NS * k:512 + NS * (k + 1)].rearrange("p (b t) -> p b t", t=TS)
                            ins = dve.tensor_copy(dst, src)
                        ins.then_inc(ql_rd, 1)
                if u == 1 and not last:
                    read_k(p + 1)
                normalise(h, u, 4)
                if not last:
                    read_q(h + 1, v)
                if not first:
                    outputs_lo(h - 1, p + (u - 1), v)

            for u in range(2):
                dve.memset(Pr[u][:, PR_AT[4]:PR_AT[5]], 0.0)
            read_q(0, 0)
            read_k(0)
            head(0, 0, True)
            with dve.Fori(0, HEADS // 2 - 1) as i:
                head(i, 1)
                head(i + 1, 0)
            head(HEADS // 2 - 1, 1)
            outputs_lo(HEADS - 1, HEADS // 2 - 1, 1)

            def fills(n, parts):
                for at in parts:
                    f = {3: 1, 4: 3, 5: 5}[at]
                    dve.wait_ge(d_fill, n * 6 + (at + 1))
                    half = slice(512 * (f % 2), 512 * (f % 2) + 512)
                    dst = CT[:, f // 2, half] if f < 4 else CTR[64:P, half]
                    bank = 512 * (4 + at % 2)
                    dve.tensor_copy(dst, ps[P - dst.shape[0]:P, bank:bank + 512]).then_inc(d_fd, 1)

            def turned(b):
                dve.wait_ge(d_pt, b + 1)
                dve.tensor_copy(PTn[:], ps[0:NS, 3584:3584 + ROWS]).then_inc(d_pd, 1)

            def latent_out(b):
                dve.wait_ge(d_o, b + 1)
                dve.tensor_copy(OL[:, 1, :, bass.ds(b, 1), :].rearrange("p h a t -> p h (a t)"),
                                ps[:, 3712:3712 + ROWS].rearrange("p (h t) -> p h t", t=TS)).then_inc(d_od, 1)

            def sample(b, more=True):
                first = isinstance(b, int) and b == 0
                if not first:
                    turned(b - 1)
                    latent_out(b - 1)
                dve.wait_ge(d_s, b + 1)
                dve.tensor_reduce(mx[0:ROWS, 0:1], ps[0:ROWS, 0:PAST + NS], AX.X, ALU.max, negate=True).then_inc(d_max, 1)
                if more:
                    fills(b + 1, (3, 4, 5))
                dve.wait_ge(d_exp, b + 1)
                dve.reciprocal(rsum[0:ROWS, 2:3], rsum[0:ROWS, 0:1]).then_inc(d_inv, 1)
                dve.wait_ge(d_inv, b + 1)
                dve.tensor_scalar(Ps[0:ROWS, :], Ps[0:ROWS, :], rsum[0:ROWS, 2:3], None, ALU.mult).then_inc(d_nrm, 1)

            dve.memset(Ps[64:P, 0:P], 0.0)
            fills(0, (3, 4, 5))
            sample(0)
            with dve.Fori(0, 2) as i:
                for s in range(3):
                    sample(i * 3 + (s + 1))
            split(C_WO, C_WO % 2, W_D)
            sample(B - 1, False)
            turned(B - 1)
            latent_out(B - 1)
            dve.wait_ge(d_vh, 1)
            dve.tensor_tensor(xl[:, :, NP:T], ps[:, 0:KD * NS].rearrange("p (k t) -> p k t", k=KD),
                              xh[:, :, NP:T].bitcast(F32), ALU.subtract).then_inc(d_vl, 1)

            def residual(c, j, u, w, scale):
                if not (isinstance(c, int) and c + 1 == C_END):
                    split_next(c, u, w)
                for s, (done, free) in enumerate(((t0_ok, f0_ok), (t1_ok, f1_ok))):
                    dve.wait_ge(done, c + 1)
                    x = xT[:, bass.ds(j * 2 + s, 1), :].rearrange("p a (h c) -> p (a h) c", h=2)
                    if scale:
                        ins = dve.scalar_tensor_tensor(x, x, ALPHA, pair(s), ALU.mult, ALU.add)
                    else:
                        ins = dve.tensor_tensor(x, x, pair(s), ALU.add)
                    ins.then_inc(free, 1)

            def last_residuals(c, n, scale):
                def shift(k):
                    dve.tensor_tensor(halves(xT[:, k, :]), halves(xT[:, k, :]), pair(2), ALU.subtract).then_inc(n_dev, 1)

                for k in range(4, KD):
                    cc, (done, free) = c + (k - 4) // 2, ((t0_ok, f0_ok), (t1_ok, f1_ok))[k % 2]
                    if k % 2 == 0 and cc + 1 < C_END:
                        split_next(cc, 0, 0)
                    dve.wait_ge(done, cc + 1)
                    x = halves(xT[:, k, :])
                    if scale:
                        ins = dve.scalar_tensor_tensor(x, x, ALPHA, pair(k % 2), ALU.mult, ALU.add)
                    else:
                        ins = dve.tensor_tensor(x, x, pair(k % 2), ALU.add)
                    ins.then_inc(free, 1)
                    if k == 4:
                        dve.wait_ge(n_mean, n + 1)
                        for e in range(EARLY):
                            shift(e)
                    dve.wait_ge(free, cc + 1)
                    shift(k)
                    if k == 6:
                        dve.wait_ge(n_sq, KD * n + 6)
                        dve.wait_ge(n_ssq, 5 * n + 4)
                        dve.tensor_tensor(ssq[:], ssq[:], sq[1][:], ALU.add).then_inc(n_ssq, 1)

            for j in range(2):
                residual(C_WO + j, j, 0, 0, True)
            last_residuals(C_WO + 2, 0, True)

            def norm(n, final=False):
                def centre(k):
                    dve.tensor_tensor(xT[:, k, :], xT[:, k, :], acc[:], ALU.subtract).then_inc(n_ctr, 1)

                dve.wait_ge(n_rcp, n + 1)
                centre(0)
                dve.wait_ge(n_var, n + 1)
                dve.wait_ge(n_rsq, n + 1)
                dve.scalar_tensor_tensor(halves(stat[:, 0, :]), pair(3), EPS, halves(stat[:, 1, :]), ALU.add,
                                         ALU.subtract).then_inc(n_eps, 1)
                centre(1)
                dve.wait_ge(n_root, n + 1)
                dve.reciprocal(stat[:, 0, :], stat[:, 1, :]).then_inc(n_inv, 1)
                dve.wait_ge(n_inv, n + 1)
                dve.wait_ge(n_ctr, 2 * n + 2)
                for k in range(KD + 1):
                    if k < KD:
                        if k >= 2:
                            dve.wait_ge(n_ctrp, (KD - 2) * n + k - 1)
                        g = V_G + KD * n + k
                        dve.scalar_tensor_tensor(xT[:, k, :], xT[:, k, :], vec[:, g:g + 1], stat[:, 0, :],
                                                 ALU.mult, ALU.mult).then_inc(n_t, 1)
                    if k >= 1 and not final:
                        dve.wait_ge(n_hi, KD * n + k)
                        g = V_B + KD * n + k - 1
                        dve.scalar_tensor_tensor(xl[:, k - 1, :], xT[:, k - 1, :], vec[:, g:g + 1],
                                                 xh[:, k - 1, :].bitcast(F32), ALU.add, ALU.subtract).then_inc(n_lo, 1)

            def up(layer, half, c, j, q, u):
                split_next(c, u, W_D)
                dve.wait_ge(f0_ok, c + 1)
                dve.wait_ge(t1_ok, c + 1)
                dve.tensor_tensor(halves(ht[u][:]), halves(sg[u][:]), pair(1), ALU.mult).then_inc(f1_ok, 1)
                dve.wait_ge(m_h, j + (layer * 2 + half) * FH + 1)
                row = lambda t: t[:, bass.ds(j, 1), :].rearrange("p a t -> p (a t)")
                dve.tensor_tensor(row(hl), ht[u][:], row(hh).bitcast(F32), ALU.subtract).then_inc(m_l, 1)

            def ffn(base, layer):
                for half in range(2):
                    b0 = base + 15 * half
                    chunk_loop(dve, b0, FH, lambda c, j, q, u: up(layer, half, c, j, q, u))
                    if half == 0:
                        dve.wait_ge(n_x, (2 * layer + 1) * KD)
                    for j in range(4 if half == 0 else 2):
                        residual(b0 + FH + j, j, 0, 0, half == 0)
                last_residuals(base + 28, 2 * layer + 1, False)

            norm(0)
            dve.wait_ge(s_lout[0], 96)
            dve.wait_ge(s_lout[1], 64)
            dve.wait_ge(s_lout[2], 32)
            ffn(*FFN[0])
            norm(1)

            def gated(j, u):
                dve.wait_ge(r_ge, j * 2 + 2)
                dve.scalar_tensor_tensor(ix[u][:, 0:NP], gr[u][:, 1, 0:NP], 1.0, xc[:, 0:NP],
                                         ALU.add, ALU.mult).then_inc(r_ix, 1)
                b = lambda t: t.rearrange("p (b s) -> p b s", b=B)
                dve.scalar_tensor_tensor(b(ix[u][:, NP:T]), b(gr[u][:, 1, NP:T]), 1.0, samples_of(xc),
                                         ALU.add, ALU.mult).then_inc(r_ix, 1)
                dve.wait_ge(r_a, j + 1)
                dve.wait_ge(r_ix, j * 2 + 2)
                dve.tensor_tensor(gr[u][:, 1, :], av[u][:], av[u][:], ALU.mult).then_inc(r_a2, 1)
                dve.wait_ge(r_th, j + 1)
                dve.wait_ge(r_a2, j + 1)
                dve.scalar_tensor_tensor(th[u][:], gr[u][:, 1, :], 1.0, th[u][:], ALU.add, ALU.mult).then_inc(r_v, 1)

            def scaled(j, u):
                dve.wait_ge(r_sq, j + 1)
                dve.tensor_tensor(ix[u][:], th[u][:], ix[u][:], ALU.mult).then_inc(r_u, 1)

            def scan(j, u):
                dve.wait_ge(r_u, j + 1)
                if above_zero(j):
                    dve.wait_ge(r_hh, j)
                dve.tensor_tensor_scan(hs[:], av[u][:, 0:NP], ix[u][:, 0:NP], 0.0, ALU.mult, ALU.add).then_inc(r_s, 1)
                dve.wait_ge(r_sm, j * 3 + 3)
                flat = lambda t: t[:].rearrange("p b s -> p (b s)")
                dve.tensor_tensor_scan(flat(h2), flat(as2), flat(us2), 0.0, ALU.mult, ALU.add).then_inc(r_s2, 1)
                dve.wait_ge(r_s, j + 1)
                dve.tensor_tensor(gel[u][:, 0:NP], hs[:], gel[u][:, 0:NP], ALU.mult).then_inc(r_y, 1)
                dve.wait_ge(r_s2, j + 1)
                g = gel[u][:, NP:T].rearrange("p (b s) -> p b s", b=B)
                dve.tensor_tensor(g, h2[:, :, 1:TS + 1], g, ALU.mult).then_inc(r_y, 1)

            def outputs_lo_part(j, u):
                dve.wait_ge(r_yh, j + 1)
                row = lambda t: t[:, bass.ds(j, 1), :].rearrange("p a t -> p (a t)")
                dve.tensor_tensor(row(yl), gel[u][:], row(yh).bitcast(F32), ALU.subtract).then_inc(r_yl, 1)

            def lru(c, j, q, u):
                if above_zero(j):
                    gated(j - 1, 1 - u)
                if above_zero(j - 1):
                    outputs_lo_part(j - 2, u)
                split_next(c, u, W_LRU)
                for n in range(1, CONV):
                    dve.wait_ge(r_x0, j + 1)
                    if n > 1:
                        dve.wait_ge(r_cv, j * 3 + (n - 1))
                    dve.scalar_tensor_tensor(xc[:, 0:UL - 3], U[u][:, n:n + UL - 3], vec[:, bass.ds(j + (V_CW + KD * n), 1)],
                                             xc[:, 0:UL - 3],
                                             ALU.mult, ALU.add).then_inc(r_cv, 1)
                if above_zero(j):
                    scaled(j - 1, 1 - u)
                dve.wait_ge(r_xh, j + 1)
                dve.tensor_tensor(xcl[:, 0:NP], xc[:, 0:NP], xch[:, 0:NP].bitcast(F32), ALU.subtract)
                dve.tensor_tensor(xcl[:, NP:T].rearrange("p (b s) -> p b s", b=B), samples_of(xc),
                                  xch[:, NP:T].rearrange("p (b s) -> p b s", b=B).bitcast(F32),
                                  ALU.subtract).then_inc(r_xl, 1)
                if above_zero(j):
                    scan(j - 1, 1 - u)

            chunk_loop(dve, C_LRU, KD, lru, head=2)
            last = (KD - 1 + C_LRU) % 2
            gated(KD - 1, last)
            outputs_lo_part(KD - 2, 1 - last)
            scaled(KD - 1, last)
            scan(KD - 1, last)
            outputs_lo_part(KD - 1, last)
            dve.wait_ge(r_t, 1)
            dve.tensor_copy(hrow[:, 512:1024], ps[0:36, 2560:3072]).then_inc(r_te, 1)
            dve.wait_ge(n_x, 2 * KD)
            for j in range(2):
                residual(C_LO + j, j, 0, 0, True)
            last_residuals(C_LO + 2, 2, True)
            norm(2)
            ffn(*FFN[1])
            norm(3, True)
            for t in range(5):
                n = P if t < 4 else NS
                dve.wait_ge(y_t, t + 1)
                if t >= 2:
                    dve.wait_ge(y_out[t % 2], 16 * (t // 2))
                dve.tensor_copy(yrow[t % 2][0:n, 512:1024],
                                ps[0:n, 1024 * (t % 2) + 512:1024 * (t % 2) + 1024]).then_inc(y_d, 1)

        @block.gpsimd
        def _(pool):
            pool.wait_ge(in_cst, 32)
            pool.wait_ge(in_id, 16)
            pool.tensor_copy(identb[:], ident[:]).then_inc(s_cb, 1)
            pool.tensor_copy(maskb[:], cst[:, 0:P]).then_inc(s_cb, 1)
            pool.tensor_copy(smaskb[:].rearrange("r b s -> r (b s)"), cst[:, P:P + B * NS]).then_inc(s_cb, 1)
            pool.wait_ge(s_kr, 3)
            pool.wait_ge(s_cb, 3)
            for s in range(2):
                pool.tensor_copy(K[s][64:P, :], krs[64:P, 0:NP]).then_inc(s_kp2, 1)
            for t in range(6):
                pool.wait_ge(s_lte, t + 1)
                n = P if t < 4 else META
                if t < 5:
                    src, s = lat[t % 2], t % 2
                    a, b = latent_prompt[0, 0, P * t:P * t + n, :], krope_prompt[0, 0, P * t:P * t + n, :]
                else:
                    src, s, n = cnew, 2, NS
                    a, b = latent_sample[0].rearrange("b t c -> (b t) c"), krope_sample[0].rearrange("b t c -> (b t) c")
                pool.dma_start(a, src[0:n, 0:KV_R]).then_inc(s_lout[s], 16)
                pool.dma_start(b, src[0:n, KV_R:KV_R + ROPE]).then_inc(s_lout[s], 16)

            def swap(u):
                pool.tensor_copy(wq[u][:, :, 96:112], wq[u][:, :, 80:96]).then_inc(wq_sw, 1)
                pool.tensor_copy(wq[u][:, :, 112:128], wq[u][:, :, 64:80]).then_inc(wq_sw, 1)

            def values(h, u):
                pool.tensor_copy(Vs[u][:, 0:4, :], V[:, 0:4, bass.ds(h * VH, VH)]).then_inc(v_cp, 1)
                pool.tensor_copy(Vs[u][0:META, 4, :], V[0:META, 4, bass.ds(h * VH, VH)]).then_inc(v_cp, 1)

            def rotary(h, u):
                pool.wait_ge(q_dve, h + 1)
                pool.wait_ge(q_act, h + 1)
                pool.tensor_copy(qrot[:, :, bass.ds(h, 1), :].rearrange("p b a t -> p b (a t)"),
                                 Q[u][:, NP:T].rearrange("p (b t) -> p b t", t=TS)).then_inc(q_rot, 1)

            pool.wait_ge(s_kp2, 2)
            for u in range(2):
                pool.wait_ge(wq_in[u], 16)
                swap(u)
            pool.wait_ge(s_ve, 5)
            pool.wait_ge(s_vd, 5)
            for u in range(2):
                values(u, u)
            with pool.Fori(0, HEADS // 2 - 1) as i:
                for u in range(2):
                    pool.wait_ge(wq_in[u], i * 16 + 32)
                    rotary(i * 2 + u, u)
                    swap(u)
                    pool.wait_ge(o_sum, i * 2 + (u + 1))
                    values(i * 2 + (u + 2), u)
            for u in range(2):
                rotary(HEADS - 2 + u, u)

            def sample_q(b, u):
                pool.tensor_copy(qs[u][:], qlat[:, :, bass.ds(b, 1), :, :].rearrange("p k a h t -> p k (a h t)")).then_inc(d_q, 1)
                pool.tensor_copy(qrs[u][:], qrot[:, bass.ds(b, 1), :, :].rearrange("p a h t -> p (a h t)")).then_inc(d_q, 1)

            pool.wait_ge(o_lo, HEADS)
            pool.wait_ge(ql_rd, HEADS)
            pool.wait_ge(q_rot, HEADS)
            for u in range(2):
                sample_q(u, u)
            with pool.Fori(0, 2) as i:
                for s in range(3):
                    pool.wait_ge(d_s, i * 3 + s)
                    sample_q(i * 3 + (s + 2), (s + 2) % 3)

            def total(base, n):
                for k in range(1, EARLY):
                    c = base + k // 2
                    pool.wait_ge(f0_ok, c + 1)
                    if k % 2:
                        pool.wait_ge(f1_ok, c + 1)
                    if k > 1:
                        pool.wait_ge(n_acc, EARLY * n + k - 1)
                    pool.tensor_tensor(acc[:], xT[:, 0, :] if k == 1 else acc[:], xT[:, k, :], ALU.add).then_inc(n_acc, 1)
                for k in range(1, 5):
                    pool.wait_ge(n_sq, KD * n + k + 1)
                    if k > 1:
                        pool.wait_ge(n_ssq, 5 * n + k - 1)
                    pool.tensor_tensor(ssq[:], ssq[:], sq[k % 2][:], ALU.add).then_inc(n_ssq, 1)
                pool.wait_ge(n_dev, KD * n + 6)
                pool.tensor_tensor(acc[:], xT[:, 4, :], xT[:, 5, :], ALU.add).then_inc(n_acc, 1)
                pool.wait_ge(n_rcp, n + 1)
                for k in range(2, KD):
                    pool.tensor_tensor(xT[:, k, :], xT[:, k, :], acc[:], ALU.subtract).then_inc(n_ctrp, 1)

            def bias(n):
                for k in range(KD):
                    pool.wait_ge(n_hi, KD * n + k + 1)
                    pool.wait_ge(n_lo, KD * (n + 1) + k + 1)
                    g = V_B + KD * n + k
                    pool.tensor_scalar(xT[:, k, :], xT[:, k, :], vec[:, g:g + 1], None, ALU.add).then_inc(n_x, 1)

            total(C_WO, 0)
            bias(0)
            total(C_FF0 + 26, 1)
            bias(1)

            for u in range(2):
                pool.memset(U[u][:, 0:3], 0.0)
            pool.memset(as2[:, :, 0:1], 0.0).then_inc(r_z, 1)

            def pads(j, u):
                if above_zero(j - 1):
                    pool.wait_ge(r_cv, j * 3 - 3)
                pool.tensor_copy(U[u][:, UP:UL].rearrange("p (b s) -> p b s", b=B)[:, :, 0:3],
                                 stT[:, bass.ds(j, 1), 0:24].rearrange("p a (b s) -> p (a b) s", b=B)).then_inc(r_pad, 1)

            def history(c, j, u):
                pool.wait_ge(f0_ok, c + 1)
                pool.tensor_copy(hist[:, bass.ds(j, 1), 0:3].rearrange("p a s -> p (a s)"), U[u][:, UP - 3:UP])
                pool.tensor_copy(hist[:, bass.ds(j, 1), 3:27].rearrange("p a (b s) -> p (a b) s", b=B),
                                 U[u][:, UP:UL].rearrange("p (b s) -> p b s", b=B)[:, :, 4:7]).then_inc(r_hc, 1)

            def states(j, u):
                pool.wait_ge(r_u, j + 1)
                if above_zero(j):
                    pool.wait_ge(r_s2, j)
                b = lambda t: t.rearrange("p (b s) -> p b s", b=B)
                pool.tensor_copy(us2[:, :, 0:1].rearrange("p b a -> p (a b)"),
                                 stT[:, bass.ds(j, 1), 24:32].rearrange("p a b -> p (a b)")).then_inc(r_sm, 1)
                pool.tensor_copy(as2[:, :, 1:TS + 1], b(av[u][:, NP:T])).then_inc(r_sm, 1)
                pool.tensor_copy(us2[:, :, 1:TS + 1], b(ix[u][:, NP:T])).then_inc(r_sm, 1)
                pool.wait_ge(r_s, j + 1)
                pool.wait_ge(r_s2, j + 1)
                pool.tensor_copy(hist[:, bass.ds(j, 1), 27:28].rearrange("p a s -> p (a s)"), hs[:, NP - 1:NP])
                pool.tensor_copy(hist[:, bass.ds(j, 1), 28:36].rearrange("p a s -> p (a s)"),
                                 h2[:, :, TS:TS + 1].rearrange("p b a -> p (b a)")).then_inc(r_hh, 1)

            def outputs_hi_part(j, u):
                pool.wait_ge(r_y, j * 2 + 2)
                pool.tensor_copy(yh[:, bass.ds(j, 1), :].rearrange("p a t -> p (a t)"), gel[u][:]).then_inc(r_yh, 1)

            def lru(c, j, q, u):
                pads(j, u)
                history(c, j, u)
                if above_zero(j):
                    states(j - 1, 1 - u)
                    outputs_hi_part(j - 1, 1 - u)

            chunk_loop(pool, C_LRU, KD, lru, head=2)
            states(KD - 1, (KD - 1 + C_LRU) % 2)
            outputs_hi_part(KD - 1, (KD - 1 + C_LRU) % 2)
            pool.wait_ge(r_te, 2)
            pool.dma_start(conv_prompt[0, 0], hrow[0:3, :]).then_inc(r_out, 16)
            pool.dma_start(conv_sample[0].rearrange("b j d -> (b j) d"), hrow[3:27, :]).then_inc(r_out, 16)
            pool.dma_start(h_prompt[0], hrow[27:28, :]).then_inc(r_out, 16)
            pool.dma_start(h_sample[0], hrow[28:36, :]).then_inc(r_out, 16)
            total(C_LO, 2)
            bias(2)
            total(C_FF1 + 26, 3)
            pool.wait_ge(r_out, 64)
            pool.wait_ge(s_lout[0], 96)
            pool.wait_ge(s_lout[1], 64)
            pool.wait_ge(s_lout[2], 32)


def constants():
    half = ROPE // 2
    freqs = np.float32(10000.0) ** (-np.arange(half, dtype=np.float32) / np.float32(half))
    pos = np.concatenate([np.arange(NP), np.tile(PAST + np.arange(TS), B)]).astype(np.float32)
    ang = (pos[:, None] * freqs[None, :]).astype(np.float32)
    cos, sin = np.cos(ang).T, np.sin(ang).T
    rot = np.concatenate([cos, cos, -sin, sin], axis=0)
    trig = np.concatenate([rot, rot * np.float32(SCALE)], axis=0).astype(np.float32)
    q, k = np.arange(P)[:, None], np.arange(P)[None, :]
    mask = np.where(k > q, np.float32(NEG), np.float32(0)).astype(np.float32)
    rows = np.arange(P)[:, None, None] % TS
    own = np.arange(B)[None, :, None]
    new = np.arange(NS)[None, None, :]
    seen = (new // TS == own) & (new % TS <= rows)
    smask = np.where(seen, np.float32(0), np.float32(NEG)).astype(np.float32).reshape(P, B * NS)
    return {"c_ident": np.eye(P, dtype=np.float32), "c_trig": trig, "c_mask": mask, "c_smask": smask}


_INS = ["x_prompt", "x_sample", "cache_latent", "cache_krope", "page_table", "state_lru_h", "state_conv",
        "meta_tokens", "mla_w_in", "mla_q_norm", "mla_w_q_up", "mla_kv_norm", "mla_w_uk", "mla_w_uv", "mla_w_o",
        "lru_w_in", "lru_conv_w", "lru_conv_b", "lru_w_a", "lru_b_a", "lru_w_i", "lru_b_i", "lru_lambda", "lru_w_o",
        "ffn_w_gu", "ffn_w_down", "ln_g", "ln_b"]
_OUTS = [(1, SEQ, D), (B, TS, D), (1, 1, NP, KV_R), (1, 1, NP, ROPE), (1, B, TS, KV_R), (1, B, TS, ROPE),
         (1, 1, D), (1, 1, CONV - 1, D), (1, B, D), (1, B, CONV - 1, D)]


def kernel(**inputs):
    import concourse.bacc as _bacc
    from concourse.bass_utils import run_bass_kernel_spmd as _run

    nc = _bacc.Bacc("TRN2", target_bir_lowering=False, num_devices=1)
    arrays, args = {}, []
    for name in _INS:
        arrays[f"in_{name}"] = np.ascontiguousarray(inputs[name])
    for name, a in constants().items():
        arrays[f"in_{name}"] = a
    for name, a in arrays.items():
        args.append(nc.dram_tensor(name, a.shape, mybir.dt.from_np(a.dtype), kind="ExternalInput").ap())
    for i, shape in enumerate(_OUTS):
        args.append(nc.dram_tensor(f"out_{i}", shape, F32, kind="ExternalOutput").ap())
    trunk(nc, *args)
    r = _run(nc, [arrays], core_ids=[0])
    return tuple(r.results[0][f"out_{i}"] for i in range(len(_OUTS)))
```

```python
from contextlib import ExitStack

import numpy as np

import concourse.bass as bass
from concourse import mybir

F32 = mybir.dt.float32
F32R = mybir.dt.float32r
BF16 = mybir.dt.bfloat16
I32 = mybir.dt.int32
ALU = mybir.AluOpType
ACT = mybir.ActivationFunctionType
AX = mybir.AxisListType

P = 128
D = 1024
KD = D // P
SEQ, META = 512, 16
NP = SEQ + META
B, TS = 8, 4
NS = B * TS
T = NP + NS
TH = T // 2
HEADS, NOPE, ROPE, VH = 16, 64, 32, 64
QL_R, KV_R = 384, 256
KQ, KC = QL_R // P, KV_R // P
PAST, PAGE = 1024, 128
PAGES = PAST // PAGE
ROWS = HEADS * TS
ROWS_AT = ((0,), (1,), (2, 3), (4, 5), ())
FF = 2816
FT = FF // P
FH = FT // 2
CONV = 4
ALPHA = (2 * 2) ** 0.25
SCALE = (NOPE + ROPE) ** -0.5
EPS = 1e-5
LRU_C = 8.0
EARLY = 4
NEG = -1.0e30
PR_AT = (0, 128, 384, 768, 1280, 1808)
XR = T // 5
UP = 3 + NP
UL = UP + B * (3 + TS)

V_G, V_B, V_CW = 0, 32, 64
V_CB, V_BA, V_BI, V_LAM, V_QN, V_KN = 96, 104, 112, 120, 128, 131
NV = 133

C_IN = 0
C_WO = 3
C_FF0 = 7
C_LRU = 37
C_LO = 45
C_FF1 = 49
C_END = 79
W_MAX = FH * 2 * P
W_D = KD * 2 * P
W_LRU = W_D + 2 * P


def chunk_cols(c):
    if C_LRU <= c < C_LO:
        return W_LRU
    for base in (C_FF0, C_FF1):
        if base <= c < base + 30 and (c - base) % 15 >= FH:
            return W_MAX
    return W_D


def chunk_loop(eng, base, n, body, head=0, tail=1):
    pairs = (n - head - tail) // 2
    for j in range(head):
        body(base + j, j, (base + j) // 2, (base + j) % 2)
    if pairs == 1:
        for j in range(head, head + 2):
            body(base + j, j, (base + j) // 2, (base + j) % 2)
    elif pairs > 1:
        with eng.Fori(0, pairs) as i:
            for s in range(2):
                first = base + head + s
                body(i * 2 + first, i * 2 + (head + s), i + first // 2, first % 2)
    for j in range(head + 2 * pairs, n):
        body(base + j, j, (base + j) // 2, (base + j) % 2)


def above_zero(v):
    return not isinstance(v, int) or v > 0


def trunk(nc, x_prompt, x_sample, cache_latent, cache_krope, page_table, state_lru_h, state_conv, meta_tokens,
          mla_w_in, mla_q_norm, mla_w_q_up, mla_kv_norm, mla_w_uk, mla_w_uv, mla_w_o,
          lru_w_in, lru_conv_w, lru_conv_b, lru_w_a, lru_b_a, lru_w_i, lru_b_i, lru_lambda, lru_w_o,
          ffn_w_gu, ffn_w_down, ln_g, ln_b, c_ident, c_trig, c_mask, c_smask,
          y_prompt, y_sample, latent_prompt, krope_prompt, latent_sample, krope_sample,
          h_prompt, conv_prompt, h_sample, conv_sample):
    N_POOL = cache_latent.shape[1]
    with ExitStack() as ctx:
        top = [(nc.sbuf_base + 63) // 64 * 64]

        def place(name, shape, dt, at):
            size = int(np.prod(shape[1:])) * (2 if dt == BF16 else 4)
            return nc.alloc_sbuf_tensor_at(name, shape, dt, offset=at), at + (size + 31) // 32 * 32

        def sb(name, shape, dt=F32):
            t, top[0] = place(name, shape, dt, top[0])
            return t

        def area(at, end):
            pos = [at]

            def put(name, shape, dt=F32):
                t, pos[0] = place(name, shape, dt, pos[0])
                assert pos[0] <= end, (name, pos[0], end)
                return t
            put.at = lambda: pos[0]
            return put

        xT = sb("xT", [P, KD, T])
        xh = sb("xh", [P, KD, T], F32R)
        xl = sb("xl", [P, KD, T], F32R)
        raw = [sb(f"raw{s}", [P, W_MAX]) for s in range(2)]
        ident = sb("ident", [P, P])
        ones = sb("ones", [P, 4, P])
        identb = sb("identb", [P, P], BF16)
        maskb = sb("maskb", [P, P], BF16)
        smaskb = sb("smaskb", [P, B, NS], BF16)
        vec = sb("vec", [P, NV])
        spare = sb("spare", [P, 1])
        hvec = sb("hvec", [P, 16])
        cdec = sb("cdec", [P, 2, KD])
        stT = sb("stT", [P, KD, 32])
        stat = sb("stat", [P, 2, T])
        ring_at = top[0]
        wh = [sb(f"wh{s}", [P, W_MAX], F32R) for s in range(2)]
        wl = [sb(f"wl{s}", [P, W_MAX], F32R) for s in range(2)]
        ring_end = top[0]
        reg = top[0]
        LIMIT = nc.sbuf_top

        put = area(reg, LIMIT)
        z = put("z", [P, KQ + KC, T])
        krs = put("krs", [P, T])
        trig = put("trig", [P, T])
        pages = put("pages", [1, B * PAGES], I32)
        wuv = put("wuv", [P, KC, HEADS * VH])
        wq = [put(f"wq{s}", [P, KQ, P]) for s in range(2)]
        wuk = put("wuk", [P, KC, P])
        heads_at = put.at()
        K = [put(f"K{s}", [P, NP]) for s in range(2)]
        Q = [put(f"Q{s}", [P, T]) for s in range(2)]
        Vs = [put(f"Vs{s}", [P, 5, VH]) for s in range(2)]
        zsq = area(heads_at, put.at())("zsq", [P, KQ + KC, T])
        rt = put("rt", [32, 2, T])
        assert put.at() - heads_at >= 4 * PAGES * (KV_R + 2 * ROPE)
        lat = [put(f"lat{s}", [P, KV_R + ROPE]) for s in range(2)]
        cnew = put("cnew", [NS, KV_R + ROPE])
        qlat = put("qlat", [P, KC, B, HEADS, TS])
        qrot = put("qrot", [P, B, HEADS, TS])
        wukT = [put(f"wukT{s}", [NOPE, KV_R]) for s in range(2)]
        mx = put("mx", [P, 2])
        rsum = put("rsum", [P, 4])
        Ctok = [put(f"Ctok{s}", [P, PAGES, KV_R + 2 * ROPE]) for s in range(2)]
        Ctok.append(area(heads_at, LIMIT)("Ctok2", [P, PAGES, KV_R + 2 * ROPE]))
        OL = put("OL", [P, KC, HEADS, B, TS])
        put = area(LIMIT - 28672, LIMIT)
        xin = put("xin", [XR, 5, D])
        prow = put("prow", [P, 2, P])
        srow = put("srow", [32, D])
        cst = put("cst", [P, P + B * NS])
        spt = put("spt", [P, 6, KD])
        put = area(ring_at, ring_end)
        V = put("V", [P, 5, HEADS * VH])
        Pr = [put(f"Pr{s}", [P, PR_AT[5]]) for s in range(2)]
        PT = put("PT", [P, 4, NP])
        PT4 = put("PT4", [META, META])
        put = area(ring_at, ring_at + 4 * W_MAX)
        CT = put("CT", [P, KC, PAST])
        qs = [put(f"qs{s}", [P, KC, ROWS]) for s in range(3)]
        qrs = [put(f"qrs{s}", [P, ROWS]) for s in range(3)]
        PTn = put("PTn", [NS, ROWS])
        put = area(ring_at + 8 * W_MAX, ring_at + 12 * W_MAX)
        CTR = put("CTR", [P, PAST])
        Ps = put("Ps", [P, PAST + NS])
        PTs = put("PTs", [P, PAGES, ROWS])
        put = area(reg, LIMIT)
        hh = put("hh", [P, FH, T], F32R)
        hl = put("hl", [P, FH, T], F32R)
        sg = [put(f"sg{s}", [P, T]) for s in range(2)]
        ht = [put(f"ht{s}", [P, T]) for s in range(2)]
        sq = [put(f"sq{s}", [P, T]) for s in range(2)]
        ssq = put("ssq", [P, T])
        acc = put("acc", [P, T])
        put = area(reg, LIMIT)
        yh = put("yh", [P, KD, T], F32R)
        yl = put("yl", [P, KD, T], F32R)
        U = [put(f"U{s}", [P, UL]) for s in range(2)]
        gel = [put(f"gel{s}", [P, T]) for s in range(2)]
        th = [put(f"th{s}", [P, T]) for s in range(2)]
        av = [put(f"av{s}", [P, T]) for s in range(2)]
        ix = [put(f"ix{s}", [P, T]) for s in range(2)]
        xc = [put(f"xc{s}", [P, UL]) for s in range(2)]
        xch = put("xch", [P, T], F32R)
        xcl = put("xcl", [P, T], F32R)
        hs = put("hs", [P, NP])
        hist = put("hist", [P, KD, 36])
        as2 = put("as2", [P, B, TS + 1])
        us2 = put("us2", [P, B, TS + 1])
        h2 = put("h2", [P, B, TS + 1])
        gr = [put(f"gr{s}", [P, 2, T]) for s in range(2)]
        put = area(LIMIT - 4160, LIMIT)
        hrow = put("hrow", [36, D])
        put = area(reg, LIMIT)
        yrow = [put(f"yrow{s}", [P, D]) for s in range(5)]

        ps = ctx.enter_context(nc.psum_tensor("ps", [P, 8 * 512], F32))

        def pair(j, lo=0, hi=P):
            return ps[lo:hi, 1024 * j:1024 * j + 1024].rearrange("p (h c) -> p h c", h=2)[:, :, 0:TH]

        def halves(ap):
            return ap.rearrange("p (h c) -> p h c", h=2)

        def samples_of(t):
            return t[:, UP:UL].rearrange("p (b s) -> p b s", b=B)[:, :, 0:TS]

        def sem(name):
            return ctx.enter_context(nc.semaphore(name))

        raw_in = [sem("raw_in0"), sem("raw_in1")]
        hi_ok, lo_ok = sem("hi_ok"), sem("lo_ok")
        t0_ok, t1_ok = sem("t0_ok"), sem("t1_ok")
        f0_ok, f1_ok = sem("f0_ok"), sem("f1_ok")
        in_x = [sem(f"in_x{t}") for t in range(5)]
        in_id, in_par, in_st, in_cst, in_att = (sem(n) for n in ("in_id", "in_par", "in_st", "in_cst", "in_att"))
        in_pg = sem("in_pg")
        s_ones, s_xt, s_xe, s_xea, s_xh0 = (sem(n) for n in ("ones_ok", "x_turned", "x_read_dve", "x_read_act", "x_hi"))
        s_pt_, s_pte, s_stt, s_ste = (sem(n) for n in ("par_turned", "par_read", "st_turned", "st_read"))
        s_par, s_parA, s_cb = sem("par_step"), sem("par_act"), sem("masks_ok")
        s_zsq, s_zms, s_zeps, s_zroot, s_zinv, s_z, s_kr, s_kp2 = (sem(n) for n in (
            "z_sq", "z_ms", "z_eps", "z_root", "z_inv", "z_ok", "kr_step", "k_rope"))
        s_lt, s_lte, s_lout = sem("lat_turned"), sem("lat_read"), [sem(f"lat_out{s}") for s in range(3)]
        s_v, s_ve, s_vd = sem("v_sum"), sem("v_act"), sem("v_dve")
        wq_in, wuk_in = [sem("wq_in0"), sem("wq_in1")], sem("wuk_in")
        wq_sw, v_cp, q_sum, q_act, q_dve, q_rot = (sem(n) for n in ("wq_sw", "v_cp", "q_sum", "q_act", "q_dve", "q_rot"))
        k_sum, k_act, k_dve = sem("k_sum"), sem("k_act"), sem("k_dve")
        wt_sum, wt_rd, ql_sum, ql_rd = (sem(n) for n in ("wt_sum", "wt_rd", "ql_sum", "ql_rd"))
        sc_sum, sc_max, sc_exp, sc_inv, sc_nrm, pt_sum, pt_rd = (sem(n) for n in (
            "sc_sum", "sc_max", "sc_exp", "sc_inv", "sc_nrm", "pt_sum", "pt_rd"))
        o_sum, o_hi, o_lo = sem("o_sum"), sem("o_hi"), sem("o_lo")
        pg_in = [sem(f"pg_in{s}") for s in range(3)]
        d_q, d_fill, d_fa, d_fd, d_s, d_max, d_exp, d_inv, d_nrm = (sem(n) for n in (
            "d_q", "d_fill", "d_fa", "d_fd", "d_s", "d_max", "d_exp", "d_inv", "d_nrm"))
        d_pt, d_pa, d_pd, d_o, d_oa, d_od, d_v, d_vh, d_vl = (sem(n) for n in (
            "d_pt", "d_pa", "d_pd", "d_o", "d_oa", "d_od", "d_v", "d_vh", "d_vl"))
        n_acc, n_mean, n_dev, n_sq, n_var, n_eps, n_root, n_inv = (sem(n) for n in (
            "n_acc", "n_mean", "n_dev", "n_sq", "n_var", "n_eps", "n_root", "n_inv"))
        n_ssq, n_rest, n_rcp, n_rsq, n_ctr, n_ctrp = (sem(n) for n in ("n_ssq", "n_rest", "n_rcp", "n_rsq", "n_ctr", "n_ctrp"))
        n_t, n_hi, n_lo, n_x = (sem(n) for n in ("n_t", "n_hi", "n_lo", "n_x"))
        m_h, m_l = sem("m_h"), sem("m_l")
        r_pad, r_x0, r_cv, r_xh, r_xl, r_g, r_ge, r_ix, r_a, r_th, r_a2, r_v, r_sq = (
            sem("r_" + n) for n in "pad x0 cv xh xl g ge ix a th a2 v sq".split())
        r_u, r_sm, r_s, r_s2, r_y, r_yh, r_yl, r_hc, r_hh, r_z, r_t, r_te = (
            sem("r_" + n) for n in "u sm s s2 y yh yl hc hh z t te".split())
        r_out = sem("r_out")
        y_t, y_a, y_d, y_out = sem("y_t"), sem("y_a"), sem("y_d"), sem("y_out")

        block = ctx.enter_context(nc.Block())
        w4 = [(0, 2), (2, 4), (4, 6), (6, 8)]
        w4d = [(0, 3), (3, 6), (6, 9), (9, 11)]
        FFN = [(C_FF0, 0), (C_FF1, 1)]

        @block.sync
        def _(sp):
            def slot_free(c):
                if above_zero(c - 1):
                    sp.wait_ge(lo_ok, c - 1)

            def load(w, cols, c, u):
                slot_free(c)
                K_, W_ = w
                view = raw[u][:, 0:K_ * W_].rearrange("p (k n) -> p k n", k=K_)
                for k0, k1 in (w4 if K_ == KD else w4d):
                    sp.dma_start(view[:, k0:k1, :], cols(k0, k1)).then_inc(raw_in[u], 16)

            win = mla_w_in[0].rearrange("(k p) n -> p k n", p=P)
            load((KD, 256), lambda k0, k1: win[:, k0:k1, 0:256], 0, 0)
            sp.dma_start(ident[:], c_ident).then_inc(in_id, 16)
            sp.dma_start(xin[0:META, 0, :], meta_tokens).then_inc(in_x[0], 16)
            sp.dma_start(xin[META:XR, 0, :], x_prompt[0, 0:XR - META, :]).then_inc(in_x[0], 16)
            for t in range(1, 4):
                sp.dma_start(xin[:, t, :], x_prompt[0, XR * t - META:XR * (t + 1) - META, :]).then_inc(in_x[t], 16)
            sp.dma_start(xin[0:NP - 4 * XR, 4, :], x_prompt[0, 4 * XR - META:SEQ, :]).then_inc(in_x[4], 16)
            sp.dma_start(xin[NP - 4 * XR:XR, 4, :], x_sample.rearrange("b t d -> (b t) d")).then_inc(in_x[4], 16)
            load((KD, 256), lambda k0, k1: win[:, k0:k1, 256:512], 1, 1)
            for a, r, n in ((ln_g.rearrange("l s (k p) -> (l s k) p", p=P), V_G, 32),
                            (ln_b.rearrange("l s (k p) -> (l s k) p", p=P), V_B, 32),
                            (lru_conv_w[0].rearrange("j (k p) -> (j k) p", p=P), V_CW, 32)):
                sp.dma_start(prow[r:r + n, 0, :], a).then_inc(in_par, 16)
            for a, r, n in ((lru_conv_b, V_CB, 8), (lru_b_a, V_BA, 8), (lru_b_i, V_BI, 8), (lru_lambda, V_LAM, 8),
                            (mla_q_norm, V_QN, KQ), (mla_kv_norm, V_KN, KC)):
                sp.dma_start(prow[r - 96:r - 96 + n, 1, :],
                             a[0].rearrange("(k p) -> k p", p=P)).then_inc(in_par, 16)
            sp.dma_start(srow[0:24, :], state_conv[0].rearrange("b j d -> (b j) d")).then_inc(in_st, 16)
            sp.dma_start(srow[24:32, :], state_lru_h[0]).then_inc(in_st, 16)
            sp.dma_start(cst[:, 0:P], c_mask).then_inc(in_cst, 16)
            sp.dma_start(cst[:, P:P + B * NS], c_smask).then_inc(in_cst, 16)
            sp.dma_start(trig[:], c_trig).then_inc(in_att, 16)
            sp.dma_start(wuv[:], mla_w_uv[0].rearrange("(k p) h v -> p k (h v)", p=P)).then_inc(in_att, 16)
            sp.dma_start(pages[:], page_table.rearrange("b n -> (b n)").rearrange("(a n) -> a n", a=1)).then_inc(in_pg, 16)
            slot_free(2)
            last = raw[0][:, 0:W_D].rearrange("p (k n) -> p k n", k=KD)
            for d0, s0, n in ((0, 512, 160), (160, 656, 16), (176, 640, 16), (192, 0, 64)):
                sp.dma_start(last[:, :, d0:d0 + n], win[:, :, s0:s0 + n]).then_inc(raw_in[0], 16)
            wo = mla_w_o[0].rearrange("(k p) n -> p k n", p=P)
            for j in range(2):
                load((KD, 256), lambda k0, k1: wo[:, k0:k1, 256 * j:256 * j + 256], C_WO + j, (C_WO + j) % 2)

            wqv = mla_w_q_up[0].rearrange("(k p) n -> p k n", p=P)
            wukv = mla_w_uk[0].rearrange("(k p) h n -> p k (h n)", p=P)
            hw = NOPE + ROPE
            for u in range(2):
                sp.dma_start(wq[u][:, :, 0:hw], wqv[:, :, hw * u:hw * u + hw]).then_inc(wq_in[u], 16)
            sp.dma_start(wuk[:], wukv[:, :, 0:P]).then_inc(wuk_in, 16)

            def sample_pages(b, u, used=None):
                numbers = [sp.value_load(pages[0:1, bass.ds(b * PAGES + n, 1)], min_val=0, max_val=N_POOL - 1)
                           for n in range(PAGES)]
                if used is not None:
                    sp.wait_ge(d_o, used)
                for n, page in enumerate(numbers):
                    sp.dma_start(Ctok[u][:, n:n + 1, 0:KV_R],
                                 cache_latent[0, bass.ds(page, 1)].rearrange("a p c -> p a c")).then_inc(pg_in[u], 16)
                    sp.dma_start(Ctok[u][:, n, KV_R:KV_R + 2 * ROPE].rearrange("p (a c) -> p a c", a=2),
                                 cache_krope[0, bass.ds(page, 1)].rearrange("a p c -> p a c").broadcast_to(
                                     [P, 2, ROPE])).then_inc(pg_in[u], 16)

            sp.wait_ge(s_xt, KD)
            sp.wait_ge(s_pt_, 2)
            sp.wait_ge(s_stt, 1)
            sp.wait_ge(s_cb, 3)
            sp.wait_ge(s_par, 26)
            sp.wait_ge(in_pg, 16)
            for u in range(2):
                sample_pages(u, u)
            with sp.Fori(0, HEADS // 2 - 1) as i:
                for u in range(2):
                    if u == 0:
                        sp.wait_ge(wt_sum, i + 1)
                        sp.dma_start(wuk[:], wukv[:, :, bass.ds(i * P + P, P)]).then_inc(wuk_in, 16)
                    sp.wait_ge(q_sum, i * 2 + (u + 1))
                    sp.dma_start(wq[u][:, :, 0:hw], wqv[:, :, bass.ds(i * (2 * hw) + (u + 2) * hw, hw)]
                                 ).then_inc(wq_in[u], 16)
            sp.wait_ge(sc_sum, HEADS * 5)
            sp.wait_ge(q_rot, HEADS)
            sp.wait_ge(q_dve, HEADS)
            sp.wait_ge(ql_sum, HEADS)
            sp.wait_ge(o_sum, HEADS)
            with sp.Fori(0, 2) as i:
                for s in range(3):
                    sample_pages(i * 3 + (s + 2), (s + 2) % 3, used=i * 3 + s)
            for j in range(2, 4):
                load((KD, 256), lambda k0, k1: wo[:, k0:k1, 256 * j:256 * j + 256], C_WO + j, (C_WO + j) % 2)

            def load_gu(layer, half, c, j, q, u):
                gu = ffn_w_gu[layer].rearrange("(k p) n -> p k n", p=P)
                slot_free(c)
                view = raw[u][:, 0:W_D].rearrange("p (k n) -> p k n", k=KD)
                col = j * P + half * FH * P
                for k0, k1 in ((0, 4), (4, 8)):
                    sp.dma_start(view[:, k0:k1, 0:P], gu[:, k0:k1, bass.ds(col, P)]).then_inc(raw_in[u], 16)
                    sp.dma_start(view[:, k0:k1, P:2 * P], gu[:, k0:k1, bass.ds(col + FF, P)]).then_inc(raw_in[u], 16)

            def ffn(base, layer):
                for half in range(2):
                    b0 = base + 15 * half
                    chunk_loop(sp, b0, FH, lambda c, j, q, u: load_gu(layer, half, c, j, q, u))
                    dn = ffn_w_down[layer].rearrange("(k p) n -> p k n", p=P)[:, half * FH:(half + 1) * FH, :]
                    chunk_loop(sp, b0 + FH, 4, lambda c, j, q, u: load(
                        (FH, 256), lambda k0, k1: dn[:, k0:k1, bass.ds(j * 256, 256)], c, u), tail=0)

            ffn(*FFN[0])

            lin = lru_w_in[0].rearrange("(k p) n -> p k n", p=P)

            def load_lru(c, j, q, u):
                slot_free(c)
                view = raw[u][:, 0:W_D].rearrange("p (k n) -> p k n", k=KD)
                sp.dma_start(view[:, :, 0:P], lin[:, :, bass.ds(j * P, P)]).then_inc(raw_in[u], 16)
                sp.dma_start(view[:, :, P:2 * P], lin[:, :, bass.ds(j * P + D, P)]).then_inc(raw_in[u], 16)
                for n, w in enumerate((lru_w_a, lru_w_i)):
                    sp.dma_start(raw[u][:, W_D + n * P:W_D + n * P + P].rearrange("p (a n) -> p a n", a=1),
                                 w[0, bass.ds(j, 1)].rearrange("a k n -> k a n")).then_inc(raw_in[u], 16)

            chunk_loop(sp, C_LRU, KD, load_lru, tail=0)
            lo_w = lru_w_o[0].rearrange("(k p) n -> p k n", p=P)
            chunk_loop(sp, C_LO, 4, lambda c, j, q, u: load(
                (KD, 256), lambda k0, k1: lo_w[:, k0:k1, bass.ds(j * 256, 256)], c, u), tail=0)
            ffn(*FFN[1])
            for t in range(5):
                sp.wait_ge(y_a, t + 1)
                sp.wait_ge(y_d, t + 1)
                if t < 4:
                    sp.dma_start(y_prompt[0, P * t:P * t + P, :], yrow[t][:]).then_inc(y_out, 16)
                else:
                    sp.dma_start(y_sample.rearrange("b t d -> (b t) d"), yrow[4][0:NS, :]).then_inc(y_out, 16)
            sp.wait_ge(y_out, 80)

        @block.tensor
        def _(pe):
            def dense(jp, u, K_, W_, col, rh, rl, done, first=None):
                hi = wh[u][:, 0:K_ * W_].rearrange("p (k n) -> p k n", k=K_)
                lo = wl[u][:, 0:K_ * W_].rearrange("p (k n) -> p k n", k=K_)
                for k in range(K_):
                    if first is not None:
                        first(k)
                    for n, (w, x) in enumerate(((hi, rh), (hi, rl), (lo, rh))):
                        for h in range(2):
                            mm = pe.matmul(ps[:, 1024 * jp + 512 * h:1024 * jp + 512 * h + TH], w[:, k, col:col + P],
                                           x[:, k, h * TH:(h + 1) * TH], start=(k == 0 and n == 0),
                                           stop=(k == K_ - 1 and n == 2))
                mm.then_inc(done, 1)

            def side_by_side(c, u, ready, done1, before=None, x=(xh, xl)):
                pe.wait_ge(lo_ok, c + 1)
                if c:
                    pe.wait_ge(f0_ok, c)
                    pe.wait_ge(f1_ok, c)
                hi = wh[u][:, 0:W_D].rearrange("p (k n) -> p k n", k=KD)
                lo = wl[u][:, 0:W_D].rearrange("p (k n) -> p k n", k=KD)
                for k in range(KD):
                    if before is not None:
                        before(k)
                    ready(k)
                    for jp in range(2):
                        for i, (w, a) in enumerate(((hi, x[0]), (hi, x[1]), (lo, x[0]))):
                            for h in range(2):
                                mm = pe.matmul(ps[:, 1024 * jp + 512 * h:1024 * jp + 512 * h + TH],
                                               w[:, k, jp * P:jp * P + P], a[:, k, h * TH:(h + 1) * TH],
                                               start=(k == 0 and i == 0), stop=(k == KD - 1 and i == 2))
                        if k == KD - 1:
                            mm.then_inc((t0_ok, done1)[jp], 1)

            def normed(n):
                return lambda k: pe.wait_ge(n_lo, KD * n + k + 1)

            def chunk(c, u, K_, W_, rh, rl, first=None):
                pe.wait_ge(lo_ok, c + 1)
                if above_zero(c):
                    pe.wait_ge(f0_ok, c)
                dense(0, u, K_, W_, 0, rh, rl, t0_ok, first)
                if above_zero(c):
                    pe.wait_ge(f1_ok, c)
                dense(1, u, K_, W_, P, rh, rl, t1_ok)

            def total(bank, n_ones, t, start, stop):
                for h in range(2):
                    mm = pe.matmul(ps[:, bank + 512 * h:bank + 512 * h + TH], ones[:, n_ones, :],
                                   t[:, h * TH:(h + 1) * TH], start=start, stop=stop)
                return mm

            def last_chunks(c, us, K_, rh, rl, n):
                pe.wait_ge(lo_ok, c + 1)
                pe.wait_ge(f0_ok, c)
                dense(0, us[0], K_, 256, 0, rh, rl, t0_ok)
                pe.wait_ge(n_acc, EARLY * n + EARLY - 1)
                total(2048, 3, acc, True, True).then_inc(n_mean, 1)
                pe.wait_ge(f1_ok, c)
                dense(1, us[0], K_, 256, P, rh, rl, t1_ok)
                pe.wait_ge(lo_ok, c + 2)
                pe.wait_ge(f0_ok, c + 1)
                dense(0, us[1], K_, 256, 0, rh, rl, t0_ok)

                def beside(k):
                    if k == K_ - 2:
                        pe.wait_ge(n_acc, EARLY * (n + 1))
                        pe.wait_ge(f0_ok, c + 2)
                        total(0, 0, acc, True, False)
                    if k == K_ - 1:
                        pe.wait_ge(n_dev, KD * n + 7)
                        total(0, 0, xT[:, 6, :], False, False)

                pe.wait_ge(f1_ok, c + 1)
                dense(1, us[1], K_, 256, P, rh, rl, t1_ok, beside)
                pe.wait_ge(n_ssq, 5 * (n + 1))
                total(3072, 0, ssq, True, False)
                pe.wait_ge(n_sq, KD * n + 7)
                total(3072, 0, sq[0], False, False)
                pe.wait_ge(n_dev, KD * n + 8)
                total(0, 0, xT[:, 7, :], False, True).then_inc(n_rest, 1)
                pe.wait_ge(n_sq, KD * n + 8)
                total(3072, 0, sq[1], False, True).then_inc(n_var, 1)
                pe.wait_ge(n_rsq, n + 1)

            def turn_x(k):
                if 2 <= k < KD:
                    pe.wait_ge(s_xe, k - 1)
                    pe.wait_ge(s_xea, k - 1)
                for t in range(5 if k < KD else 0):
                    if k == 0:
                        pe.wait_ge(in_x[t], 16 if t in (1, 2, 3) else 32)
                    at = 1024 * (2 + k % 2) + (XR * t if t < 3 else 512 + XR * (t - 3))
                    mm = pe.transpose(ps[:, at:at + XR], xin[:, t, k * P:(k + 1) * P], ident[0:XR, 0:XR])
                    if t == 4:
                        mm.then_inc(s_xt, 1)

            pe.wait_ge(in_id, 16)
            turn_x(0)
            turn_x(1)
            side_by_side(0, 0, normed(0), t1_ok, lambda k: turn_x(k + 2))
            pe.wait_ge(s_xe, KD)
            pe.wait_ge(s_xea, KD)
            pe.wait_ge(in_par, 144)
            pe.transpose(ps[:, 2048:2048 + 96], prow[0:96, 0, :], ident[0:96, 0:96]).then_inc(s_pt_, 1)
            pe.transpose(ps[:, 2048 + 96:2048 + NV], prow[0:NV - 96, 1, :],
                         ident[0:NV - 96, 0:NV - 96]).then_inc(s_pt_, 1)
            pe.wait_ge(in_st, 32)
            for k in range(KD):
                mm = pe.transpose(ps[:, 3072 + 32 * k:3072 + 32 * k + 32], srow[:, k * P:(k + 1) * P],
                                  ident[0:32, 0:32])
            mm.then_inc(s_stt, 1)
            chunk(1, 1, KD, 256, xh, xl)

            def mean_squares(jp, tiles, o):
                for n in tiles:
                    pe.wait_ge(s_zsq, n + 1)
                    for h in range(2):
                        mm = pe.matmul(ps[:, 1024 * jp + 512 * h:1024 * jp + 512 * h + TH], ones[:, o, :],
                                       zsq[:, n, h * TH:(h + 1) * TH], start=(n == tiles[0]), stop=(n == tiles[-1]))
                mm.then_inc(s_zms, 1)

            pe.wait_ge(s_ones, 4)
            pe.wait_ge(s_pte, 1)
            pe.wait_ge(s_ste, 1)
            mean_squares(2, range(KQ), 1)
            pe.wait_ge(lo_ok, 3)
            pe.wait_ge(f0_ok, 2)
            dense(0, 0, KD, 256, 0, xh, xl, t0_ok)
            pe.wait_ge(f1_ok, 2)
            dense(1, 0, KD, 256, P, xh, xl, t1_ok,
                  lambda k: mean_squares(3, range(KQ, KQ + KC), 2) if k == 3 else None)
            pe.wait_ge(in_att, 32)
            pe.wait_ge(s_z, KQ + KC)
            pe.wait_ge(s_zeps, 2)
            g = 0
            for kt in range(5):
                n = P if kt < 4 else META
                for h in range(2):
                    if g >= 6:
                        pe.wait_ge(s_ve if g % 2 == 0 else s_vd, (g - 6) // 2 + 1)
                    bank = 512 * (2 + (g + 2) % 6)
                    for k in range(KC):
                        mm = pe.matmul(ps[0:n, bank:bank + 512], z[:, KQ + k, kt * P:kt * P + n],
                                       wuv[:, k, h * 512:(h + 1) * 512], start=(k == 0), stop=(k == KC - 1))
                    mm.then_inc(s_v, 1)
                    g += 1
                for t in ROWS_AT[kt]:
                    t0, n = (P * t, P) if t < 4 else ((SEQ, META) if t == 4 else (NP, NS))
                    if t == 0:
                        pe.wait_ge(s_kr, 3)
                    if t >= 2:
                        pe.wait_ge(s_lte, t - 1)
                    bank = 512 * (t % 2)
                    for k in range(KC):
                        pe.transpose(ps[0:n, bank + k * P:bank + (k + 1) * P], z[:, KQ + k, t0:t0 + n], ident[:])
                    pe.transpose(ps[0:n, bank + KV_R:bank + KV_R + ROPE], krs[64:96, t0:t0 + n],
                                 ident[64:96, 64:96]).then_inc(s_lt, 1)

            def keys(p):
                pe.wait_ge(wuk_in, (p + 1) * 16)
                if above_zero(p):
                    pe.wait_ge(o_lo, (p - 1) * 2)
                for h in range(2):
                    for k in range(KC):
                        mm = pe.matmul(ps[:, 512 * (6 + h):512 * (6 + h) + NP // 2], wuk[:, k, :],
                                       z[:, KQ + k, h * (NP // 2):(h + 1) * (NP // 2)], start=(k == 0), stop=(k == KC - 1))
                mm.then_inc(k_sum, 1)

            def queries(h, u, n):
                if n == 0:
                    pe.wait_ge(wq_sw, h * 2 + 2)
                for k in range(KQ):
                    mm = pe.matmul(ps[:, 512 * n:512 * n + TH], wq[u][:, k, :], z[:, k, n * TH:(n + 1) * TH],
                                   start=(k == 0), stop=(k == KQ - 1))
                if n == 1:
                    mm.then_inc(q_sum, 1)

            def scores(h, u, i):
                n = P if i < 4 else META
                bank = 512 * (2 + i % 2)
                if above_zero(h * 5 + (0, 0, 1, 2, 4)[i]):
                    pe.wait_ge(sc_exp, h * 5 + (0, 0, 1, 2, 4)[i])
                w = P * i + n
                q = Q[u][:, P * i:P * i + n]
                if i < 4:
                    pe.matmul(ps[0:n, bank:bank + w], q, K[u][:, 0:w], start=True, stop=False)
                    mm = pe.matmul(ps[0:n, bank + P * i:bank + w], identb[:], maskb[:], start=False, stop=True)
                else:
                    pe.matmul(ps[0:n, 1024:1536], q, K[u][:, 0:512], start=True, stop=True)
                    pe.matmul(ps[0:n, 1536:1536 + n], q, K[u][:, 512:NP], start=True, stop=False)
                    mm = pe.matmul(ps[0:n, 1536:1536 + n], identb[0:n, 0:n], maskb[0:n, 0:n], start=False, stop=True)
                mm.then_inc(sc_sum, 1)

            def turn(h, u, i):
                n = P if i < 4 else META
                pe.wait_ge(sc_nrm, h * 5 + (i + 1))
                if above_zero(h * 6 + max(0, i - 1)):
                    pe.wait_ge(pt_rd, h * 6 + max(0, i - 1))
                bank = 512 * (4 + i % 2)
                for j in range(i + 1):
                    kk = P if j < 4 else META
                    m = P if j == 0 else n
                    at = PR_AT[i] + j * P
                    mm = pe.transpose(ps[0:kk, bank + j * n:bank + j * n + m], Pr[u][0:m, at:at + kk],
                                      ident[0:m, 0:m])
                mm.then_inc(pt_sum, 1)

            def outputs(h, u):
                pe.wait_ge(pt_rd, h * 6 + 6)
                pe.wait_ge(v_cp, h * 2 + 2)
                if above_zero(h):
                    pe.wait_ge(o_lo, h)
                hp = NP // 2
                for j in range(5):
                    kk = P if j < 4 else META
                    for half in range(2):
                        q0 = max(P * j, half * hp)
                        q1 = (half + 1) * hp
                        if q0 >= q1:
                            continue
                        at = 512 * (6 + half) + q0 - half * hp
                        mm = pe.matmul(ps[64 * u:64 * u + VH, at:at + q1 - q0], Vs[u][0:kk, j, :],
                                       PT[:, j, q0:q1] if j < 4 else PT4[:],
                                       start=(j == 0), stop=(j == 4 or (half == 0 and j == 2)))
                mm.then_inc(o_sum, 1)

            def head(p, u, first=False):
                h, v = p * 2 + u, 1 - u
                last = isinstance(h, int) and h == HEADS - 1
                if u == 0:
                    pe.wait_ge(k_act, p + 1)
                    pe.wait_ge(k_dve, p + 1)
                pe.wait_ge(q_act, h + 1)
                pe.wait_ge(q_dve, h + 1)
                for i in range(5):
                    scores(h, u, i)
                    if not first:
                        turn(h - 1, v, i)
                    if i == 0 and u == 0:
                        for k in range(KC):
                            mm = pe.transpose(ps[:, k * P:(k + 1) * P], wuk[:, k, :], ident[:])
                        mm.then_inc(wt_sum, 1)
                    if i == 1 and u == 1 and not last:
                        keys(p + 1)
                    if i == 2:
                        pe.wait_ge(wt_rd, p + 1)
                        for k in range(KC):
                            mm = pe.matmul(ps[:, 512 + NS * k:512 + NS * (k + 1)], wukT[u][:, k * P:(k + 1) * P],
                                           Q[u][0:NOPE, NP:T], start=True, stop=True)
                        mm.then_inc(ql_sum, 1)
                    if i == 3 and not last:
                        queries(h + 1, v, 0)
                if not last:
                    pe.wait_ge(ql_rd, h + 1)
                    queries(h + 1, v, 1)
                if not first:
                    if u == 1 and not last:
                        pe.wait_ge(k_act, p + 2)
                        pe.wait_ge(k_dve, p + 2)
                    outputs(h - 1, v)

            pe.wait_ge(s_lte, 6)
            for n in range(2):
                queries(0, 0, n)
            pe.wait_ge(s_ve, 5)
            pe.wait_ge(s_vd, 5)
            keys(0)
            pe.wait_ge(s_kp2, 2)
            pe.wait_ge(s_cb, 3)
            head(0, 0, True)
            with pe.Fori(0, HEADS // 2 - 1) as i:
                head(i, 1)
                head(i + 1, 0)
            head(HEADS // 2 - 1, 1)
            for i in range(5):
                turn(HEADS - 1, 1, i)
            outputs(HEADS - 1, 1)

            def fill(n, u, f):
                at = (0, 2, 4, 1, 3, 5).index(f)
                by, count = ((d_fd, -2), (d_fd, -1), (d_fd, 0), (d_fa, 1), (d_fa, 2), (d_fa, 3))[at]
                if above_zero(n * 3 + count):
                    pe.wait_ge(by, n * 3 + count)
                bank = 512 * (4 + at % 3)
                for k in range(4):
                    pg = 4 * (f % 2) + k
                    if f < 4:
                        mm = pe.transpose(ps[:, bank + k * P:bank + (k + 1) * P],
                                          Ctok[u][:, pg, (f // 2) * P:(f // 2 + 1) * P], ident[:])
                    else:
                        mm = pe.transpose(ps[:, bank + k * P:bank + (k + 1) * P],
                                          Ctok[u][:, pg, KV_R - 64:KV_R + 64], ident[:])
                mm.then_inc(d_fill, 1)

            def sample_scores(b, u, kb, between=None):
                out = ps[0:ROWS, 512 * kb:512 * kb + (512 if kb < 2 else NS)]
                for k in range(KC):
                    rhs = CT[:, k, 512 * kb:512 * kb + 512] if kb < 2 else z[:, KQ + k, NP:T]
                    pe.matmul(out, qs[u][:, k, :], rhs, start=(k == 0), stop=False)
                    if k == 0 and between is not None:
                        between()
                rhs = CTR[64:P, 512 * kb:512 * kb + 512] if kb < 2 else krs[64:P, NP:T]
                mm = pe.matmul(out, qrs[u][64:P, :], rhs, start=False, stop=(kb < 2))
                if kb == 2:
                    pe.matmul(out, identb[:, 0:ROWS],
                              smaskb[:, b, :] if isinstance(b, int) else smaskb[:, bass.ds(b, 1), :],
                              start=False, stop=True)
                return mm

            def sample_turn(b):
                pe.wait_ge(d_nrm, b + 1)
                if not (isinstance(b, int) and b == B - 1):
                    pe.wait_ge(d_fd, b * 3 + 6)
                if above_zero(b):
                    pe.wait_ge(d_od, b)
                for k in range(PAGES):
                    m = P if k == 0 else ROWS
                    pe.transpose(ps[:, 3072 + ROWS * k:3072 + ROWS * k + m], Ps[0:m, k * P:(k + 1) * P],
                                 ident[0:m, 0:m])
                pe.transpose(ps[0:NS, 3584:3584 + ROWS], Ps[0:ROWS, PAST:PAST + NS], ident[0:ROWS, 0:ROWS]).then_inc(d_pt, 1)

            def sample_out(b, u):
                pe.wait_ge(d_pa, b + 1)
                pe.wait_ge(d_pd, b + 1)
                if above_zero(b):
                    pe.wait_ge(d_oa, b)
                for k in range(KC):
                    at = (1536, 3712)[k]
                    out = ps[:, at:at + ROWS]
                    for j in range(PAGES):
                        pe.matmul(out, Ctok[u][:, j, k * P:(k + 1) * P], PTs[:, j, :], start=(j == 0), stop=False)
                    mm = pe.matmul(out, cnew[:, k * P:(k + 1) * P], PTn[:], start=False, stop=True)
                mm.then_inc(d_o, 1)

            def sample(b, u, rounds, more=True):
                first = isinstance(b, int) and b == 0
                nu, pu = (u + 1) % 3, (u - 1) % 3
                pe.wait_ge(d_fa, b * 3 + 3)
                pe.wait_ge(d_q, b * 2 + 2)
                if not first:
                    pe.wait_ge(d_exp, b)
                sample_scores(b, u, 0)
                if not first:
                    sample_turn(b - 1)
                sample_scores(b, u, 2)
                pe.wait_ge(d_fd, b * 3 + 3)
                sample_scores(b, u, 1, None if first else lambda: sample_out(b - 1, pu)).then_inc(d_s, 1)
                if more:
                    pe.wait_ge(pg_in[nu], rounds * 256)
                    for f in (0, 2, 4, 1, 3, 5):
                        fill(b + 1, nu, f)

            pe.wait_ge(o_lo, HEADS)
            pe.wait_ge(pg_in[0], 256)
            for f in (0, 2, 4, 1, 3, 5):
                fill(0, 0, f)
            sample(0, 0, 1)
            with pe.Fori(0, 2) as i:
                for s in range(3):
                    sample(i * 3 + (s + 1), (s + 1) % 3, i + (s + 5) // 3)
            sample(B - 1, (B - 1) % 3, 0, False)

            def w_o_part(jp, h):
                u = C_WO % 2
                hi, lo = (w[u][:, 0:W_D].rearrange("p (k n) -> p k n", k=KD) for w in (wh, wl))
                at = 1024 * jp + 512 * h
                for k in range(KD):
                    for n, (w, x) in enumerate(((hi, xh), (hi, xl), (lo, xh))):
                        mm = pe.matmul(ps[:, at:at + TH], w[:, k, jp * P:jp * P + P], x[:, k, h * TH:(h + 1) * TH],
                                       start=(k == 0 and n == 0), stop=(k == KD - 1 and n == 2))
                return mm

            pe.wait_ge(lo_ok, C_WO + 1)
            pe.wait_ge(d_exp, B)
            w_o_part(0, 0)
            sample_turn(B - 1)
            w_o_part(1, 0)
            sample_out(B - 1, (B - 1) % 3)
            pe.wait_ge(d_oa, B)
            pe.wait_ge(d_od, B)
            for h in range(HEADS):
                for k in range(KC):
                    at = 2560 + NS * (h // 2)
                    mm = pe.matmul(ps[64 * (h % 2):64 * (h % 2) + VH, at:at + NS],
                                   wuv[:, k, VH * h:VH * (h + 1)], OL[:, k, h, :, :].rearrange("p b t -> p (b t)"),
                                   start=(k == 0), stop=(k == KC - 1))
            mm.then_inc(d_v, 1)

            pe.wait_ge(d_vl, 1)
            w_o_part(0, 1).then_inc(t0_ok, 1)
            w_o_part(1, 1).then_inc(t1_ok, 1)
            chunk(C_WO + 1, (C_WO + 1) % 2, KD, 256, xh, xl)
            last_chunks(C_WO + 2, (C_WO % 2, 1 - C_WO % 2), KD, xh, xl, 0)

            def ffn(base, layer, n):
                for half in range(2):
                    b0 = base + 15 * half
                    if half == 0:
                        side_by_side(b0, b0 % 2, normed(n + 1), t1_ok)
                    chunk_loop(pe, b0 + (half == 0), FH - (half == 0),
                               lambda c, j, q, u: chunk(c, u, KD, 256, xh, xl), tail=0)
                    done = (layer * 2 + half + 1) * FH

                    def hidden(k):
                        if k in (0, FH - 1):
                            pe.wait_ge(m_l, done if k else done - 1)

                    body = lambda c, j, q, u: chunk(c, u, FH, 256, hh, hl, hidden)
                    if half == 0:
                        chunk_loop(pe, b0 + FH, 4, body, tail=0)
                    else:
                        c = b0 + FH
                        for j in range(2):
                            chunk(c + j, (c + j) % 2, FH, 256, hh, hl, hidden)
                        last_chunks(c + 2, (c % 2, 1 - c % 2), FH, hh, hl, n + 1)

            ffn(C_FF0, 0, 0)

            def lru_input(c, u):
                pe.wait_ge(lo_ok, c + 1)
                pe.wait_ge(f0_ok, c)
                dense(0, u, KD, 256, 0, xh, xl, t0_ok)

            def lru_branch(c, u):
                pe.wait_ge(f1_ok, c)
                dense(1, u, KD, 256, P, xh, xl, r_g)

            def lru_gates(j, u):
                pe.wait_ge(r_xl, j + 1)
                pe.wait_ge(r_ge, j * 2)
                for g in range(2):
                    for n, (w, x) in enumerate(((wh[u], xch), (wh[u], xcl), (wl[u], xch))):
                        for h in range(2):
                            at = 1024 * (2 + g) + 512 * h
                            mm = pe.matmul(ps[:, at:at + TH], w[:, W_D + g * P:W_D + (g + 1) * P],
                                           x[:, h * TH:(h + 1) * TH], start=(n == 0), stop=(n == 2))
                mm.then_inc(t1_ok, 1)

            def lru(c, j, u):
                lru_input(c, u)
                lru_gates(j - 1, 1 - u)
                lru_branch(c, u)

            u0 = C_LRU % 2
            side_by_side(C_LRU, u0, normed(2), r_g)
            lru(C_LRU + 1, 1, 1 - u0)
            with pe.Fori(0, KD // 2 - 1) as i:
                for s in range(2):
                    c = C_LRU + 2 + s
                    lru(i * 2 + c, i * 2 + (2 + s), c % 2)
            lru_gates(KD - 1, 1 - u0)
            def histories(k):
                if k == KD - 1:
                    pe.wait_ge(r_hc, KD)
                    pe.wait_ge(r_hh, KD)
                    pe.wait_ge(r_ge, 2 * KD)
                    for n in range(KD):
                        mm = pe.transpose(ps[0:36, 2048 + n * P:2048 + (n + 1) * P], hist[:, n, :], ident[:])
                    mm.then_inc(r_t, 1)

            side_by_side(C_LO, C_LO % 2, lambda k: pe.wait_ge(r_yl, k + 1), t1_ok, histories, (yh, yl))
            chunk(C_LO + 1, (C_LO + 1) % 2, KD, 256, yh, yl)
            pe.wait_ge(r_te, 2)
            last_chunks(C_LO + 2, (C_LO % 2, 1 - C_LO % 2), KD, yh, yl, 2)
            ffn(C_FF1, 1, 2)
            pe.wait_ge(n_eps, 4)
            for k in range(KD):
                pe.wait_ge(n_hi, KD * 3 + k + 1)
                for t in range(4):
                    at = 1024 * t + k * P
                    mm = pe.transpose(ps[:, at:at + P], xT[:, k, META + P * t:META + P * t + P], ident[:])
                    if k == KD - 1:
                        mm.then_inc(y_t, 1)
            pe.wait_ge(y_a, 1)
            pe.wait_ge(y_d, 1)
            for k in range(KD):
                mm = pe.transpose(ps[0:NS, k * P:k * P + P], xT[:, k, NP:T], ident[:])
            mm.then_inc(y_t, 1)

        @block.scalar
        def _(act):
            def split(c, q, u, w):
                act.wait_ge(raw_in[u], q * 64 + 64)
                if above_zero(c - 1):
                    act.wait_ge(t1_ok, c - 1)
                act.activation(wh[u][:, 0:w], raw[u][:, 0:w], ACT.Copy).then_inc(hi_ok, 1)

            def split_next(c, q, u, w):
                if isinstance(c, int):
                    split(c + 1, (c + 1) // 2, (c + 1) % 2, chunk_cols(c + 1))
                else:
                    split(c + 1, q + u, 1 - u, w)

            split(0, 0, 0, W_D)
            for k in range(KD):
                act.wait_ge(s_xt, k + 1)
                act.activation(xT[:, k, 0:3 * XR], ps[:, 1024 * (2 + k % 2):1024 * (2 + k % 2) + 3 * XR],
                               ACT.Copy).then_inc(s_xea, 1)
                act.wait_ge(s_xe, k + 1)
                act.wait_ge(s_xea, k + 1)
                act.activation(xh[:, k, :], xT[:, k, :], ACT.Copy).then_inc(s_xh0, 1)
            split(1, 0, 1, W_D)
            for c in range(3):
                act.wait_ge(t0_ok, c + 1)
                act.activation(halves(z[:, 2 * c, :]), pair(0), ACT.Copy).then_inc(f0_ok, 1)
                act.wait_ge(f0_ok, c + 1)
                act.activation(zsq[:, 2 * c, :], z[:, 2 * c, :], ACT.Square).then_inc(s_zsq, 1)
                if c < 2:
                    act.wait_ge(f1_ok, c + 1)
                    act.activation(zsq[:, 2 * c + 1, :], z[:, 2 * c + 1, :], ACT.Square).then_inc(s_zsq, 1)
                if c == 0:
                    split(2, 1, 0, W_D)
                    act.wait_ge(s_par, 2)
                    act.activation(spt[:, 1, :], spt[:, 0, :], ACT.Exp).then_inc(s_parA, 1)
                else:
                    act.wait_ge(s_zeps, c)
                    act.activation(stat[:, c - 1, :], stat[:, c - 1, :], ACT.Sqrt).then_inc(s_zroot, 1)
            for kt in range(5):
                n = P if kt < 4 else META
                g = 2 * kt
                act.wait_ge(s_v, g + 1)
                bank = 512 * (2 + (g + 2) % 6)
                act.activation(V[0:n, kt, 0:512], ps[0:n, bank:bank + 512], ACT.Copy).then_inc(s_ve, 1)
                for t in ROWS_AT[kt]:
                    n = P if t < 4 else (META if t == 4 else NS)
                    act.wait_ge(s_lt, t + 1)
                    if t in (2, 3, 4):
                        act.wait_ge(s_lout[t % 2], 32 * (t // 2))
                    dst = lat[t % 2] if t < 5 else cnew
                    act.activation(dst[0:n, :], ps[0:n, 512 * (t % 2):512 * (t % 2) + KV_R + ROPE],
                                   ACT.Copy).then_inc(s_lte, 1)

            def exp(h, u, i):
                n = P if i < 4 else META
                w = P * i + n
                act.wait_ge(sc_max, h * 5 + (i + 1))
                act.activation(Pr[u][0:n, PR_AT[i]:PR_AT[i] + w], ps[0:n, 512 * (2 + i % 2):512 * (2 + i % 2) + w],
                               ACT.Exp, bias=mx[0:n, i % 2:i % 2 + 1],
                               accum_out=rsum[0:n, i % 2:i % 2 + 1]).then_inc(sc_exp, 1)

            def read_pt(h, i):
                n = P if i < 4 else META
                m = min(i + 1, 4)
                bank = 512 * (4 + i % 2)
                act.wait_ge(pt_sum, h * 5 + (i + 1))
                act.activation(PT[:, 0:m, P * i:P * i + n],
                               ps[:, bank:bank + m * n].rearrange("p (j q) -> p j q", j=m), ACT.Copy).then_inc(pt_rd, 1)
                if i == 4:
                    act.activation(PT4[:], ps[0:META, bank + 4 * n:bank + 5 * n], ACT.Copy).then_inc(pt_rd, 1)

            def read_k(p):
                act.wait_ge(k_sum, p + 1)
                act.activation(K[0][0:NOPE, :].rearrange("p (h c) -> p h c", h=2), pair(3, 0, 64)[:, :, 0:NP // 2],
                               ACT.Copy).then_inc(k_act, 1)

            def read_q(h, u):
                act.wait_ge(q_sum, h + 1)
                if above_zero(h - 1):
                    act.wait_ge(q_rot, h - 1)
                act.activation(halves(Q[u][0:NOPE, :]), pair(0, 0, 64), ACT.Copy, scale=SCALE).then_inc(q_act, 1)

            def outputs_hi(h, p, u):
                act.wait_ge(o_sum, h + 1)
                dst = xh[64 * u:64 * u + 64, bass.ds(p, 1), 0:NP].rearrange("p a (h c) -> p (a h) c", h=2)
                act.activation(dst, pair(3, 64 * u, 64 * u + 64)[:, :, 0:NP // 2], ACT.Copy).then_inc(o_hi, 1)

            def head(p, u, first=False):
                h, v = p * 2 + u, 1 - u
                last = isinstance(h, int) and h == HEADS - 1
                for i in range(5):
                    if i == 4 and u == 1 and not last:
                        act.wait_ge(sc_sum, h * 5 + 5)
                        read_k(p + 1)
                    exp(h, u, i)
                    if not first:
                        read_pt(h - 1, i)
                    if i == 0 and u == 0:
                        act.wait_ge(wt_sum, p + 1)
                        for s in range(2):
                            ins = act.activation(wukT[s][:], ps[64 * s:64 * s + 64, 0:KV_R], ACT.Copy)
                        ins.then_inc(wt_rd, 1)
                if not last:
                    read_q(h + 1, v)
                if not first:
                    outputs_hi(h - 1, p + (u - 1), v)

            read_q(0, 0)
            read_k(0)
            head(0, 0, True)
            with act.Fori(0, HEADS // 2 - 1) as i:
                head(i, 1)
                head(i + 1, 0)
            head(HEADS // 2 - 1, 1)
            for i in range(5):
                read_pt(HEADS - 1, i)
            outputs_hi(HEADS - 1, HEADS // 2 - 1, 1)

            def fills(n, parts):
                for at in parts:
                    f = {0: 0, 1: 2, 2: 4}[at]
                    act.wait_ge(d_fill, n * 6 + (at + 1))
                    half = slice(512 * (f % 2), 512 * (f % 2) + 512)
                    dst = CT[:, f // 2, half] if f < 4 else CTR[64:P, half]
                    bank = 512 * (4 + at % 3)
                    act.activation(dst, ps[P - dst.shape[0]:P, bank:bank + 512], ACT.Copy).then_inc(d_fa, 1)

            def turned(b):
                act.wait_ge(d_pt, b + 1)
                act.activation(PTs[:].rearrange("p j r -> p (j r)"), ps[:, 3072:3584], ACT.Copy).then_inc(d_pa, 1)

            def latent_out(b):
                act.wait_ge(d_o, b + 1)
                act.activation(OL[:, 0, :, bass.ds(b, 1), :].rearrange("p h a t -> p h (a t)"),
                               ps[:, 1536:1536 + ROWS].rearrange("p (h t) -> p h t", t=TS), ACT.Copy).then_inc(d_oa, 1)

            def sample(b, more=True):
                first = isinstance(b, int) and b == 0
                if not first:
                    turned(b - 1)
                    latent_out(b - 1)
                if more:
                    fills(b + 1, (0, 1, 2))
                act.wait_ge(d_max, b + 1)
                act.activation(Ps[0:ROWS, :], ps[0:ROWS, 0:PAST + NS], ACT.Exp, bias=mx[0:ROWS, 0:1],
                               accum_out=rsum[0:ROWS, 0:1]).then_inc(d_exp, 1)

            fills(0, (0, 1, 2))
            sample(0)
            with act.Fori(0, 2) as i:
                for s in range(3):
                    sample(i * 3 + (s + 1))
            split(C_WO, C_WO // 2, C_WO % 2, W_D)
            sample(B - 1, False)
            turned(B - 1)
            latent_out(B - 1)
            act.wait_ge(d_v, 1)
            act.activation(xh[:, :, NP:T], ps[:, 2560:2560 + KD * NS].rearrange("p (k t) -> p k t", k=KD), ACT.Copy).then_inc(d_vh, 1)
            def square(n, k):
                act.wait_ge(n_dev, KD * n + k + 1)
                if k >= 3:
                    act.wait_ge(n_ssq, 5 * n + k - 2)
                act.activation((sq[k % 2] if k else ssq)[:], xT[:, k, :], ACT.Square).then_inc(n_sq, 1)

            def splits_norm(c, n, start=0):
                for j in range(start, 3):
                    split_next(c + j, 0, 0, 0)
                for k in range(5):
                    square(n, k)
                if c + 4 < C_END:
                    split_next(c + 3, 0, 0, 0)
                for k in range(5, KD):
                    square(n, k)
                    if k == KD - 2:
                        act.activation(spare[:], ones[:, 0, 0:1], ACT.Sqrt)

            splits_norm(C_WO, 0)

            def norm(n, final=False):
                act.wait_ge(n_rest, n + 1)
                act.activation(halves(acc[:]), pair(0), ACT.Copy).then_inc(n_rcp, 1)
                act.activation(halves(stat[:, 1, :]), pair(0), ACT.Square).then_inc(n_rsq, 1)
                act.wait_ge(n_eps, n + 1)
                act.activation(stat[:, 1, :], stat[:, 0, :], ACT.Sqrt).then_inc(n_root, 1)
                for k in range(KD):
                    act.wait_ge(n_t, KD * n + k + 1)
                    bias = vec[:, V_B + KD * n + k:V_B + KD * n + k + 1]
                    dst = xT if final else xh
                    act.activation(dst[:, k, :], xT[:, k, :], ACT.Identity, bias=bias).then_inc(n_hi, 1)

            def up(base, layer, half, c, j, q, u):
                split_next(c, q, u, W_D)
                act.wait_ge(t0_ok, c + 1)
                act.activation(halves(sg[u][:]), pair(0), ACT.Silu).then_inc(f0_ok, 1)
                act.wait_ge(f1_ok, c + 1)
                act.activation(hh[:, bass.ds(j, 1), :].rearrange("p a t -> p (a t)"), ht[u][:], ACT.Copy).then_inc(m_h, 1)

            def ffn(base, layer):
                for half in range(2):
                    b0 = base + 15 * half
                    chunk_loop(act, b0, FH, lambda c, j, q, u: up(b0, layer, half, c, j, q, u))
                    if half == 0:
                        for c in range(b0 + FH, b0 + 15):
                            split_next(c, 0, 0, 0)
                splits_norm(base + 26, 2 * layer + 1)

            norm(0)
            ffn(*FFN[0])
            norm(1)

            def col(t, n, j):
                return t[:, bass.ds(j + n, 1)]

            def gates(c, j, u):
                act.wait_ge(t1_ok, c + 1)
                for g in range(2):
                    act.activation(halves(gr[u][:, g, :]), pair(2 + g), ACT.Tanh, scale=0.5,
                                   bias=col(hvec, KD * g, j)).then_inc(r_ge, 1)
                act.wait_ge(r_ge, j * 2 + 1)
                act.activation(av[u][:], gr[u][:, 0, :], ACT.Exp, scale=cdec[:, 0, bass.ds(j, 1)],
                               bias=cdec[:, 0, bass.ds(j, 1)]).then_inc(r_a, 1)
                act.activation(th[u][:], gr[u][:, 0, :], ACT.Tanh, scale=cdec[:, 1, bass.ds(j, 1)],
                               bias=cdec[:, 1, bass.ds(j, 1)]).then_inc(r_th, 1)

            def scale_of_input(j, u):
                act.wait_ge(r_v, j + 1)
                act.activation(th[u][:], th[u][:], ACT.Sqrt, scale=0.25).then_inc(r_sq, 1)

            def lru(c, j, q, u):
                if not above_zero(j):
                    split_next(c, q, u, W_LRU)
                act.wait_ge(t0_ok, c + 1)
                if above_zero(j - 1):
                    act.wait_ge(r_cv, j * 3 - 3)
                    act.wait_ge(r_hc, j - 1)
                act.activation(U[u][:, 3:3 + TH], ps[:, 0:TH], ACT.Copy)
                act.activation(U[u][:, 3 + TH:UP], ps[:, 512:512 + NP - TH], ACT.Copy)
                act.activation(U[u][:, UP:UL].rearrange("p (b s) -> p b s", b=B)[:, :, 3:7],
                               ps[:, 512 + NP - TH:512 + TH].rearrange("p (b s) -> p b s", b=B),
                               ACT.Copy).then_inc(f0_ok, 1)
                act.wait_ge(f0_ok, c + 1)
                act.wait_ge(r_pad, j + 1)
                if above_zero(j - 1):
                    act.wait_ge(r_ix, j * 2 - 2)
                act.activation(xc[u][:, 0:UL - 3], U[u][:, 0:UL - 3], ACT.Identity, scale=col(vec, V_CW, j),
                               bias=col(vec, V_CB, j)).then_inc(r_x0, 1)
                if above_zero(j):
                    split_next(c, q, u, W_LRU)
                    gates(c - 1, j - 1, 1 - u)
                act.wait_ge(r_cv, j * 3 + 3)
                act.wait_ge(t1_ok, c)
                act.activation(xch[:, 0:NP], xc[u][:, 0:NP], ACT.Copy)
                act.activation(xch[:, NP:T].rearrange("p (b s) -> p b s", b=B),
                               samples_of(xc[u]), ACT.Copy).then_inc(r_xh, 1)
                act.wait_ge(r_g, j + 1)
                if above_zero(j - 1):
                    act.wait_ge(r_yl, j - 1)
                act.activation(halves(gel[u][:]), pair(1), ACT.Gelu_apprx_tanh).then_inc(f1_ok, 1)
                if above_zero(j):
                    scale_of_input(j - 1, 1 - u)

            chunk_loop(act, C_LRU, KD, lru, head=2)
            gates(C_LRU + KD - 1, KD - 1, (KD - 1 + C_LRU) % 2)
            scale_of_input(KD - 1, (KD - 1 + C_LRU) % 2)
            split_next(C_LO, 0, 0, 0)
            act.wait_ge(r_t, 1)
            act.activation(hrow[:, 0:512], ps[0:36, 2048:2560], ACT.Copy).then_inc(r_te, 1)
            splits_norm(C_LO, 2, 1)
            norm(2)
            ffn(*FFN[1])
            norm(3, True)
            for t in range(5):
                n = P if t < 4 else NS
                act.wait_ge(y_t, t + 1)
                at = 1024 * (t % 4)
                act.activation(yrow[t][0:n, 0:512], ps[0:n, at:at + 512], ACT.Copy).then_inc(y_a, 1)

        @block.vector
        def _(dve):
            def split(c, u, w):
                dve.wait_ge(hi_ok, c + 1)
                dve.tensor_tensor(wl[u][:, 0:w], raw[u][:, 0:w], wh[u][:, 0:w].bitcast(F32),
                                  ALU.subtract).then_inc(lo_ok, 1)

            def split_next(c, u, w):
                if isinstance(c, int):
                    split(c + 1, (c + 1) % 2, chunk_cols(c + 1))
                else:
                    split(c + 1, 1 - u, w)

            for n, v in enumerate((1.0 / D, 1.0 / QL_R, 1.0 / KV_R, 1.0 / (EARLY * P))):
                dve.memset(ones[:, n, :], v).then_inc(s_ones, 1)
            split(0, 0, W_D)
            for k in range(KD + 1):
                if k < KD:
                    dve.wait_ge(s_xt, k + 1)
                    at = 1024 * (2 + k % 2) + 512
                    dve.tensor_copy(xT[:, k, 3 * XR:T], ps[:, at:at + 2 * XR]).then_inc(s_xe, 1)
                if k >= 1:
                    dve.wait_ge(s_xh0, k)
                    dve.tensor_tensor(xl[:, k - 1, :], xT[:, k - 1, :], xh[:, k - 1, :].bitcast(F32),
                                      ALU.subtract).then_inc(n_lo, 1)
            split(1, 1, W_D)

            def latents(c):
                dve.wait_ge(t1_ok, c + 1)
                dve.tensor_copy(halves(z[:, 2 * c + 1, :]), pair(1)).then_inc(f1_ok, 1)

            latents(0)
            dve.wait_ge(s_pt_, 2)
            dve.tensor_copy(vec[:], ps[:, 2048:2048 + NV]).then_inc(s_pte, 1)
            dve.wait_ge(s_stt, 1)
            dve.tensor_copy(stT[:].rearrange("p k r -> p (k r)"), ps[:, 3072:3072 + 32 * KD]).then_inc(s_ste, 1)
            steps = [0]

            def step(ins):
                steps[0] += 1
                ins.then_inc(s_par, 1)
                dve.wait_ge(s_par, steps[0])

            lam = vec[:, V_LAM:V_LAM + KD]
            neg, y, s2, ser, den, sv = (spt[:, n, :] for n in range(6))
            dve.wait_ge(s_pte, 1)
            step(dve.tensor_scalar(s2, lam, -1.0, None, ALU.mult))
            step(dve.tensor_tensor(neg, lam, s2, ALU.min))
            split(2, 0, W_D)
            dve.wait_ge(s_parA, 1)
            step(dve.tensor_scalar(den, y, 2.0, None, ALU.add))
            step(dve.reciprocal(sv, den))
            step(dve.tensor_tensor(sv, sv, y, ALU.mult))
            step(dve.tensor_tensor(s2, sv, sv, ALU.mult))
            step(dve.tensor_scalar(ser, s2, 1.0 / 17, 1.0 / 15, ALU.mult, ALU.add))
            for d in (13, 11, 9, 7, 5, 3, 1):
                step(dve.tensor_tensor(ser, ser, s2, ALU.mult))
                step(dve.tensor_scalar(ser, ser, 1.0 / d, None, ALU.add))
            step(dve.tensor_tensor(ser, ser, sv, ALU.mult))
            step(dve.tensor_scalar(s2, lam, -1.0, 0.0, ALU.mult, ALU.max))
            step(dve.scalar_tensor_tensor(s2, ser, 2.0, s2, ALU.mult, ALU.add))
            step(dve.tensor_scalar(cdec[:, 0, :], s2, -LRU_C / 2, None, ALU.mult))
            step(dve.tensor_scalar(cdec[:, 1, :], s2, LRU_C / 2, None, ALU.mult))
            dve.tensor_scalar(hvec[:], vec[:, V_BA:V_BA + 16], 0.5, None, ALU.mult).then_inc(s_par, 1)

            latents(1)
            for n, tiles in enumerate((range(KQ), range(KQ, KQ + KC))):
                dve.wait_ge(s_zms, n + 1)
                dve.tensor_scalar(halves(stat[:, n, :]), pair(2 + n), EPS, None, ALU.add).then_inc(s_zeps, 1)
                dve.wait_ge(s_zroot, n + 1)
                dve.reciprocal(stat[:, n, :], stat[:, n, :]).then_inc(s_zinv, 1)
                dve.wait_ge(s_zinv, n + 1)
                for k in tiles:
                    g = V_QN + k
                    dve.scalar_tensor_tensor(z[:, k, :], z[:, k, :], vec[:, g:g + 1], stat[:, n, :],
                                             ALU.mult, ALU.mult).then_inc(s_z, 1)
            dve.wait_ge(in_att, 32)
            dve.wait_ge(t1_ok, 3)
            dve.tensor_tensor(halves(rt[:, 0, :]), pair(1, 0, 32), halves(trig[0:32, :]), ALU.mult).then_inc(s_kr, 1)
            dve.tensor_tensor(halves(rt[:, 1, :]), pair(1, 32, 64), halves(trig[32:64, :]), ALU.mult).then_inc(f1_ok, 1)
            dve.wait_ge(f1_ok, 3)
            dve.wait_ge(s_kr, 1)
            for r in (64, 96):
                dve.tensor_tensor(krs[r:r + 32, :], rt[:, 0, :], rt[:, 1, :], ALU.add).then_inc(s_kr, 1)
            for g in range(1, 10, 2):
                kt, h = g // 2, g % 2
                n = P if kt < 4 else META
                dve.wait_ge(s_v, g + 1)
                bank = 512 * (2 + (g + 2) % 6)
                dve.tensor_copy(V[0:n, kt, h * 512:(h + 1) * 512], ps[0:n, bank:bank + 512]).then_inc(s_vd, 1)

            def top_score(h, i):
                n = P if i < 4 else META
                w = P * i + n
                dve.wait_ge(sc_sum, h * 5 + (i + 1))
                dve.tensor_reduce(mx[0:n, i % 2:i % 2 + 1], ps[0:n, 512 * (2 + i % 2):512 * (2 + i % 2) + w], AX.X,
                                  ALU.max, negate=True).then_inc(sc_max, 1)

            def normalise(h, u, i):
                n = P if i < 4 else META
                w = P * i + n
                dve.wait_ge(sc_exp, h * 5 + (i + 1))
                dve.reciprocal(rsum[0:n, 2 + i % 2:3 + i % 2], rsum[0:n, i % 2:i % 2 + 1]).then_inc(sc_inv, 1)
                dve.wait_ge(sc_inv, h * 5 + (i + 1))
                p = Pr[u][0:n, PR_AT[i]:PR_AT[i] + w]
                dve.tensor_scalar(p, p, rsum[0:n, 2 + i % 2:3 + i % 2], None, ALU.mult).then_inc(sc_nrm, 1)

            def read_k(p):
                dve.wait_ge(k_sum, p + 1)
                dve.tensor_copy(K[1][0:NOPE, :].rearrange("p (h c) -> p h c", h=2),
                                pair(3, 64, P)[:, :, 0:NP // 2]).then_inc(k_dve, 1)

            def read_q(h, u):
                dve.wait_ge(q_sum, h + 1)
                if above_zero(h - 1):
                    dve.wait_ge(q_rot, h - 1)
                dve.tensor_tensor(halves(Q[u][64:P, :]), pair(0, 64, P), halves(trig[64:P, :]), ALU.mult).then_inc(q_dve, 1)

            def outputs_lo(h, p, u):
                dve.wait_ge(o_hi, h + 1)
                rows = slice(64 * u, 64 * u + 64)
                dst = xl[rows, bass.ds(p, 1), 0:NP].rearrange("p a (h c) -> p (a h) c", h=2)
                hi = xh[rows, bass.ds(p, 1), 0:NP].rearrange("p a (h c) -> p (a h) c", h=2)
                dve.tensor_tensor(dst, pair(3, 64 * u, 64 * u + 64)[:, :, 0:NP // 2], hi.bitcast(F32),
                                  ALU.subtract).then_inc(o_lo, 1)

            def head(p, u):
                h, v = p * 2 + u, 1 - u
                last = isinstance(h, int) and h == HEADS - 1
                for i in range(5):
                    top_score(h, i)
                    if i == 4 and u == 1 and not last:
                        read_k(p + 1)
                    if i == 0 and above_zero(p):
                        outputs_lo(h - 2, p - 1, u)
                    if i >= 1:
                        normalise(h, u, i - 1)
                    if i == 2:
                        dve.wait_ge(ql_sum, h + 1)
                        for k in range(KC):
                            dst = qlat[:, k, :, bass.ds(h, 1), :].rearrange("p b a t -> p b (a t)")
                            src = ps[:, 512 + NS * k:512 + NS * (k + 1)].rearrange("p (b t) -> p b t", t=TS)
                            ins = dve.tensor_copy(dst, src)
                        ins.then_inc(ql_rd, 1)
                normalise(h, u, 4)
                if not last:
                    read_q(h + 1, v)

            for u in range(2):
                dve.memset(Pr[u][:, PR_AT[4]:PR_AT[5]], 0.0)
            read_q(0, 0)
            read_k(0)
            for u in range(2):
                head(0, u)
            with dve.Fori(1, HEADS // 2 - 1) as i:
                for u in range(2):
                    head(i, u)
            for u in range(2):
                head(HEADS // 2 - 1, u)
            for u in range(2):
                outputs_lo(HEADS - 2 + u, HEADS // 2 - 1, u)

            def fills(n, parts):
                for at in parts:
                    f = {3: 1, 4: 3, 5: 5}[at]
                    dve.wait_ge(d_fill, n * 6 + (at + 1))
                    half = slice(512 * (f % 2), 512 * (f % 2) + 512)
                    dst = CT[:, f // 2, half] if f < 4 else CTR[64:P, half]
                    bank = 512 * (4 + at % 3)
                    dve.tensor_copy(dst, ps[P - dst.shape[0]:P, bank:bank + 512]).then_inc(d_fd, 1)

            def turned(b):
                dve.wait_ge(d_pt, b + 1)
                dve.tensor_copy(PTn[:], ps[0:NS, 3584:3584 + ROWS]).then_inc(d_pd, 1)

            def latent_out(b):
                dve.wait_ge(d_o, b + 1)
                dve.tensor_copy(OL[:, 1, :, bass.ds(b, 1), :].rearrange("p h a t -> p h (a t)"),
                                ps[:, 3712:3712 + ROWS].rearrange("p (h t) -> p h t", t=TS)).then_inc(d_od, 1)

            def sample(b, more=True):
                first = isinstance(b, int) and b == 0
                if not first:
                    turned(b - 1)
                    latent_out(b - 1)
                dve.wait_ge(d_s, b + 1)
                dve.tensor_reduce(mx[0:ROWS, 0:1], ps[0:ROWS, 0:PAST + NS], AX.X, ALU.max, negate=True).then_inc(d_max, 1)
                if more:
                    fills(b + 1, (3, 4, 5))
                dve.wait_ge(d_exp, b + 1)
                dve.reciprocal(rsum[0:ROWS, 2:3], rsum[0:ROWS, 0:1]).then_inc(d_inv, 1)
                dve.wait_ge(d_inv, b + 1)
                dve.tensor_scalar(Ps[0:ROWS, :], Ps[0:ROWS, :], rsum[0:ROWS, 2:3], None, ALU.mult).then_inc(d_nrm, 1)

            dve.memset(Ps[64:P, 0:P], 0.0)
            fills(0, (3, 4, 5))
            sample(0)
            with dve.Fori(0, 2) as i:
                for s in range(3):
                    sample(i * 3 + (s + 1))
            split(C_WO, C_WO % 2, W_D)
            sample(B - 1, False)
            turned(B - 1)
            latent_out(B - 1)
            dve.wait_ge(d_vh, 1)
            dve.tensor_tensor(xl[:, :, NP:T], ps[:, 2560:2560 + KD * NS].rearrange("p (k t) -> p k t", k=KD),
                              xh[:, :, NP:T].bitcast(F32), ALU.subtract).then_inc(d_vl, 1)

            def residual(c, j, u, w, scale, next_split=True):
                if next_split:
                    split_next(c, u, w)
                for s, (done, free) in enumerate(((t0_ok, f0_ok), (t1_ok, f1_ok))):
                    dve.wait_ge(done, c + 1)
                    x = xT[:, bass.ds(j * 2 + s, 1), :].rearrange("p a (h c) -> p (a h) c", h=2)
                    if scale:
                        ins = dve.scalar_tensor_tensor(x, x, ALPHA, pair(s), ALU.mult, ALU.add)
                    else:
                        ins = dve.tensor_tensor(x, x, pair(s), ALU.add)
                    ins.then_inc(free, 1)

            def last_residuals(c, n, scale):
                def shift(k):
                    dve.tensor_tensor(halves(xT[:, k, :]), halves(xT[:, k, :]), pair(2), ALU.subtract).then_inc(n_dev, 1)

                for k in range(4, KD):
                    cc, (done, free) = c + (k - 4) // 2, ((t0_ok, f0_ok), (t1_ok, f1_ok))[k % 2]
                    if k % 2 == 0 and cc + 1 < C_END:
                        split_next(cc, 0, 0)
                    dve.wait_ge(done, cc + 1)
                    x = halves(xT[:, k, :])
                    if scale:
                        ins = dve.scalar_tensor_tensor(x, x, ALPHA, pair(k % 2), ALU.mult, ALU.add)
                    else:
                        ins = dve.tensor_tensor(x, x, pair(k % 2), ALU.add)
                    ins.then_inc(free, 1)
                    if k == 4:
                        dve.wait_ge(n_mean, n + 1)
                        for e in range(EARLY):
                            shift(e)
                    dve.wait_ge(free, cc + 1)
                    shift(k)
                    if k == 6:
                        dve.wait_ge(n_sq, KD * n + 6)
                        dve.wait_ge(n_ssq, 5 * n + 4)
                        dve.tensor_tensor(ssq[:], ssq[:], sq[1][:], ALU.add).then_inc(n_ssq, 1)

            for j in range(2):
                residual(C_WO + j, j, 0, 0, True)
            last_residuals(C_WO + 2, 0, True)

            def norm(n, final=False):
                def centre(k):
                    dve.tensor_tensor(xT[:, k, :], xT[:, k, :], acc[:], ALU.subtract).then_inc(n_ctr, 1)

                dve.wait_ge(n_rcp, n + 1)
                centre(0)
                dve.wait_ge(n_var, n + 1)
                dve.wait_ge(n_rsq, n + 1)
                dve.scalar_tensor_tensor(halves(stat[:, 0, :]), pair(3), EPS, halves(stat[:, 1, :]), ALU.add,
                                         ALU.subtract).then_inc(n_eps, 1)
                centre(1)
                dve.wait_ge(n_root, n + 1)
                dve.reciprocal(stat[:, 0, :], stat[:, 1, :]).then_inc(n_inv, 1)
                dve.wait_ge(n_inv, n + 1)
                dve.wait_ge(n_ctr, 2 * n + 2)
                for k in range(KD + 1):
                    if k < KD:
                        if k >= 2:
                            dve.wait_ge(n_ctrp, (KD - 2) * n + k - 1)
                        g = V_G + KD * n + k
                        dve.scalar_tensor_tensor(xT[:, k, :], xT[:, k, :], vec[:, g:g + 1], stat[:, 0, :],
                                                 ALU.mult, ALU.mult).then_inc(n_t, 1)
                    if k >= 1 and not final:
                        dve.wait_ge(n_hi, KD * n + k)
                        g = V_B + KD * n + k - 1
                        dve.scalar_tensor_tensor(xl[:, k - 1, :], xT[:, k - 1, :], vec[:, g:g + 1],
                                                 xh[:, k - 1, :].bitcast(F32), ALU.add, ALU.subtract).then_inc(n_lo, 1)

            def up(layer, half, c, j, q, u):
                split_next(c, u, W_D)
                dve.wait_ge(f0_ok, c + 1)
                dve.wait_ge(t1_ok, c + 1)
                dve.tensor_tensor(halves(ht[u][:]), halves(sg[u][:]), pair(1), ALU.mult).then_inc(f1_ok, 1)
                dve.wait_ge(m_h, j + (layer * 2 + half) * FH + 1)
                row = lambda t: t[:, bass.ds(j, 1), :].rearrange("p a t -> p (a t)")
                dve.tensor_tensor(row(hl), ht[u][:], row(hh).bitcast(F32), ALU.subtract).then_inc(m_l, 1)

            def ffn(base, layer):
                for half in range(2):
                    b0 = base + 15 * half
                    chunk_loop(dve, b0, FH, lambda c, j, q, u: up(layer, half, c, j, q, u))
                    if half == 0:
                        dve.wait_ge(n_x, (2 * layer + 1) * KD)
                    for j in range(4 if half == 0 else 2):
                        residual(b0 + FH + j, j, 0, 0, half == 0)
                last_residuals(base + 28, 2 * layer + 1, False)

            norm(0)
            dve.wait_ge(s_lout[0], 96)
            dve.wait_ge(s_lout[1], 64)
            dve.wait_ge(s_lout[2], 32)
            ffn(*FFN[0])
            norm(1)

            def gated(j, u):
                dve.wait_ge(r_ge, j * 2 + 2)
                dve.scalar_tensor_tensor(ix[u][:, 0:NP], gr[u][:, 1, 0:NP], 1.0, xc[u][:, 0:NP],
                                         ALU.add, ALU.mult).then_inc(r_ix, 1)
                b = lambda t: t.rearrange("p (b s) -> p b s", b=B)
                dve.scalar_tensor_tensor(b(ix[u][:, NP:T]), b(gr[u][:, 1, NP:T]), 1.0, samples_of(xc[u]),
                                         ALU.add, ALU.mult).then_inc(r_ix, 1)
                dve.wait_ge(r_a, j + 1)
                dve.wait_ge(r_ix, j * 2 + 2)
                dve.tensor_tensor(gr[u][:, 1, :], av[u][:], av[u][:], ALU.mult).then_inc(r_a2, 1)
                dve.wait_ge(r_th, j + 1)
                dve.wait_ge(r_a2, j + 1)
                dve.scalar_tensor_tensor(th[u][:], gr[u][:, 1, :], 1.0, th[u][:], ALU.add, ALU.mult).then_inc(r_v, 1)

            def scaled(j, u):
                dve.wait_ge(r_sq, j + 1)
                dve.tensor_tensor(ix[u][:], th[u][:], ix[u][:], ALU.mult).then_inc(r_u, 1)

            def scan(j, u):
                dve.wait_ge(r_u, j + 1)
                if above_zero(j):
                    dve.wait_ge(r_hh, j)
                dve.tensor_tensor_scan(hs[:], av[u][:, 0:NP], ix[u][:, 0:NP], 0.0, ALU.mult, ALU.add).then_inc(r_s, 1)
                dve.wait_ge(r_sm, j * 3 + 3)
                flat = lambda t: t[:].rearrange("p b s -> p (b s)")
                dve.tensor_tensor_scan(flat(h2), flat(as2), flat(us2), 0.0, ALU.mult, ALU.add).then_inc(r_s2, 1)
                dve.wait_ge(r_s, j + 1)
                dve.tensor_tensor(gel[u][:, 0:NP], hs[:], gel[u][:, 0:NP], ALU.mult).then_inc(r_y, 1)
                dve.wait_ge(r_s2, j + 1)
                g = gel[u][:, NP:T].rearrange("p (b s) -> p b s", b=B)
                dve.tensor_tensor(g, h2[:, :, 1:TS + 1], g, ALU.mult).then_inc(r_y, 1)

            def outputs_lo_part(j, u):
                dve.wait_ge(r_yh, j + 1)
                row = lambda t: t[:, bass.ds(j, 1), :].rearrange("p a t -> p (a t)")
                dve.tensor_tensor(row(yl), gel[u][:], row(yh).bitcast(F32), ALU.subtract).then_inc(r_yl, 1)

            def lru(c, j, q, u):
                if not above_zero(j):
                    split_next(c, u, W_LRU)
                x = xc[u][:, 0:UL - 3]
                for n in range(1, CONV):
                    dve.wait_ge(r_x0, j + 1)
                    if n > 1:
                        dve.wait_ge(r_cv, j * 3 + (n - 1))
                    dve.scalar_tensor_tensor(x, U[u][:, n:n + UL - 3], vec[:, bass.ds(j + (V_CW + KD * n), 1)], x,
                                             ALU.mult, ALU.add).then_inc(r_cv, 1)
                if above_zero(j):
                    split_next(c, u, W_LRU)
                if above_zero(j - 1):
                    outputs_lo_part(j - 2, u)
                if above_zero(j):
                    gated(j - 1, 1 - u)
                dve.wait_ge(r_xh, j + 1)
                dve.tensor_tensor(xcl[:, 0:NP], xc[u][:, 0:NP], xch[:, 0:NP].bitcast(F32), ALU.subtract)
                dve.tensor_tensor(xcl[:, NP:T].rearrange("p (b s) -> p b s", b=B), samples_of(xc[u]),
                                  xch[:, NP:T].rearrange("p (b s) -> p b s", b=B).bitcast(F32),
                                  ALU.subtract).then_inc(r_xl, 1)
                if above_zero(j):
                    scaled(j - 1, 1 - u)
                    scan(j - 1, 1 - u)

            chunk_loop(dve, C_LRU, KD, lru, head=2)
            last = (KD - 1 + C_LRU) % 2
            gated(KD - 1, last)
            scaled(KD - 1, last)
            outputs_lo_part(KD - 2, 1 - last)
            scan(KD - 1, last)
            outputs_lo_part(KD - 1, last)
            split_next(C_LO, 0, 0)
            dve.wait_ge(r_t, 1)
            dve.tensor_copy(hrow[:, 512:1024], ps[0:36, 2560:3072]).then_inc(r_te, 1)
            dve.wait_ge(n_x, 2 * KD)
            for j in range(2):
                residual(C_LO + j, j, 0, 0, True, j > 0)
            last_residuals(C_LO + 2, 2, True)
            norm(2)
            ffn(*FFN[1])
            norm(3, True)
            for t in range(5):
                n = P if t < 4 else NS
                dve.wait_ge(y_t, t + 1)
                at = 1024 * (t % 4) + 512
                dve.tensor_copy(yrow[t][0:n, 512:1024], ps[0:n, at:at + 512]).then_inc(y_d, 1)

        @block.gpsimd
        def _(pool):
            pool.wait_ge(in_cst, 32)
            pool.wait_ge(in_id, 16)
            pool.tensor_copy(identb[:], ident[:]).then_inc(s_cb, 1)
            pool.tensor_copy(maskb[:], cst[:, 0:P]).then_inc(s_cb, 1)
            pool.tensor_copy(smaskb[:].rearrange("r b s -> r (b s)"), cst[:, P:P + B * NS]).then_inc(s_cb, 1)
            pool.wait_ge(s_kr, 3)
            pool.wait_ge(s_cb, 3)
            for s in range(2):
                pool.tensor_copy(K[s][64:P, :], krs[64:P, 0:NP]).then_inc(s_kp2, 1)
            for t in range(6):
                pool.wait_ge(s_lte, t + 1)
                n = P if t < 4 else META
                if t < 5:
                    src, s = lat[t % 2], t % 2
                    a, b = latent_prompt[0, 0, P * t:P * t + n, :], krope_prompt[0, 0, P * t:P * t + n, :]
                else:
                    src, s, n = cnew, 2, NS
                    a, b = latent_sample[0].rearrange("b t c -> (b t) c"), krope_sample[0].rearrange("b t c -> (b t) c")
                pool.dma_start(a, src[0:n, 0:KV_R]).then_inc(s_lout[s], 16)
                pool.dma_start(b, src[0:n, KV_R:KV_R + ROPE]).then_inc(s_lout[s], 16)

            def swap(u):
                pool.tensor_copy(wq[u][:, :, 96:112], wq[u][:, :, 80:96]).then_inc(wq_sw, 1)
                pool.tensor_copy(wq[u][:, :, 112:128], wq[u][:, :, 64:80]).then_inc(wq_sw, 1)

            def values(h, u):
                pool.tensor_copy(Vs[u][:, 0:4, :], V[:, 0:4, bass.ds(h * VH, VH)]).then_inc(v_cp, 1)
                pool.tensor_copy(Vs[u][0:META, 4, :], V[0:META, 4, bass.ds(h * VH, VH)]).then_inc(v_cp, 1)

            def rotary(h, u):
                pool.wait_ge(q_dve, h + 1)
                pool.wait_ge(q_act, h + 1)
                pool.tensor_copy(qrot[:, :, bass.ds(h, 1), :].rearrange("p b a t -> p b (a t)"),
                                 Q[u][:, NP:T].rearrange("p (b t) -> p b t", t=TS)).then_inc(q_rot, 1)

            pool.wait_ge(s_kp2, 2)
            for u in range(2):
                pool.wait_ge(wq_in[u], 16)
                swap(u)
            pool.wait_ge(s_ve, 5)
            pool.wait_ge(s_vd, 5)
            for u in range(2):
                values(u, u)
            with pool.Fori(0, HEADS // 2 - 1) as i:
                for u in range(2):
                    pool.wait_ge(wq_in[u], i * 16 + 32)
                    rotary(i * 2 + u, u)
                    swap(u)
                    pool.wait_ge(o_sum, i * 2 + (u + 1))
                    values(i * 2 + (u + 2), u)
            for u in range(2):
                rotary(HEADS - 2 + u, u)

            def sample_q(b, u):
                pool.tensor_copy(qs[u][:], qlat[:, :, bass.ds(b, 1), :, :].rearrange("p k a h t -> p k (a h t)")).then_inc(d_q, 1)
                pool.tensor_copy(qrs[u][:], qrot[:, bass.ds(b, 1), :, :].rearrange("p a h t -> p (a h t)")).then_inc(d_q, 1)

            pool.wait_ge(o_lo, HEADS)
            pool.wait_ge(ql_rd, HEADS)
            pool.wait_ge(q_rot, HEADS)
            for u in range(2):
                sample_q(u, u)
            with pool.Fori(0, 2) as i:
                for s in range(3):
                    pool.wait_ge(d_s, i * 3 + s)
                    sample_q(i * 3 + (s + 2), (s + 2) % 3)

            def total(base, n):
                for k in range(1, EARLY):
                    c = base + k // 2
                    pool.wait_ge(f0_ok, c + 1)
                    if k % 2:
                        pool.wait_ge(f1_ok, c + 1)
                    if k > 1:
                        pool.wait_ge(n_acc, EARLY * n + k - 1)
                    pool.tensor_tensor(acc[:], xT[:, 0, :] if k == 1 else acc[:], xT[:, k, :], ALU.add).then_inc(n_acc, 1)
                for k in range(1, 5):
                    pool.wait_ge(n_sq, KD * n + k + 1)
                    if k > 1:
                        pool.wait_ge(n_ssq, 5 * n + k - 1)
                    pool.tensor_tensor(ssq[:], ssq[:], sq[k % 2][:], ALU.add).then_inc(n_ssq, 1)
                pool.wait_ge(n_dev, KD * n + 6)
                pool.tensor_tensor(acc[:], xT[:, 4, :], xT[:, 5, :], ALU.add).then_inc(n_acc, 1)
                pool.wait_ge(n_rcp, n + 1)
                for k in range(2, KD):
                    pool.tensor_tensor(xT[:, k, :], xT[:, k, :], acc[:], ALU.subtract).then_inc(n_ctrp, 1)

            def bias(n, tiles=range(KD)):
                for k in tiles:
                    pool.wait_ge(n_hi, KD * n + k + 1)
                    pool.wait_ge(n_lo, KD * (n + 1) + k + 1)
                    g = V_B + KD * n + k
                    pool.tensor_scalar(xT[:, k, :], xT[:, k, :], vec[:, g:g + 1], None, ALU.add).then_inc(n_x, 1)

            total(C_WO, 0)
            bias(0)
            total(C_FF0 + 26, 1)

            for u in range(2):
                pool.memset(U[u][:, 0:3], 0.0)
            pool.memset(as2[:, :, 0:1], 0.0).then_inc(r_z, 1)

            def pads(j, u):
                if above_zero(j - 1):
                    pool.wait_ge(r_cv, j * 3 - 3)
                pool.tensor_copy(U[u][:, UP:UL].rearrange("p (b s) -> p b s", b=B)[:, :, 0:3],
                                 stT[:, bass.ds(j, 1), 0:24].rearrange("p a (b s) -> p (a b) s", b=B)).then_inc(r_pad, 1)

            def history(c, j, u):
                pool.wait_ge(f0_ok, c + 1)
                pool.tensor_copy(hist[:, bass.ds(j, 1), 0:3].rearrange("p a s -> p (a s)"), U[u][:, UP - 3:UP])
                pool.tensor_copy(hist[:, bass.ds(j, 1), 3:27].rearrange("p a (b s) -> p (a b) s", b=B),
                                 U[u][:, UP:UL].rearrange("p (b s) -> p b s", b=B)[:, :, 4:7]).then_inc(r_hc, 1)

            def states(j, u):
                pool.wait_ge(r_u, j + 1)
                if above_zero(j):
                    pool.wait_ge(r_s2, j)
                b = lambda t: t.rearrange("p (b s) -> p b s", b=B)
                pool.tensor_copy(us2[:, :, 0:1].rearrange("p b a -> p (a b)"),
                                 stT[:, bass.ds(j, 1), 24:32].rearrange("p a b -> p (a b)")).then_inc(r_sm, 1)
                pool.tensor_copy(as2[:, :, 1:TS + 1], b(av[u][:, NP:T])).then_inc(r_sm, 1)
                pool.tensor_copy(us2[:, :, 1:TS + 1], b(ix[u][:, NP:T])).then_inc(r_sm, 1)
                pool.wait_ge(r_s, j + 1)
                pool.wait_ge(r_s2, j + 1)
                pool.tensor_copy(hist[:, bass.ds(j, 1), 27:28].rearrange("p a s -> p (a s)"), hs[:, NP - 1:NP])
                pool.tensor_copy(hist[:, bass.ds(j, 1), 28:36].rearrange("p a s -> p (a s)"),
                                 h2[:, :, TS:TS + 1].rearrange("p b a -> p (b a)")).then_inc(r_hh, 1)

            def outputs_hi_part(j, u):
                pool.wait_ge(r_y, j * 2 + 2)
                pool.tensor_copy(yh[:, bass.ds(j, 1), :].rearrange("p a t -> p (a t)"), gel[u][:]).then_inc(r_yh, 1)

            def lru(c, j, q, u):
                if not above_zero(j):
                    pads(j, u)
                history(c, j, u)
                if not (isinstance(j, int) and j == KD - 1):
                    pads(j + 1, 1 - u)
                if isinstance(j, int) and j < 2:
                    bias(1, range(4 * j, 4 * j + 4))
                if above_zero(j):
                    states(j - 1, 1 - u)
                    outputs_hi_part(j - 1, 1 - u)

            chunk_loop(pool, C_LRU, KD, lru, head=2)
            states(KD - 1, (KD - 1 + C_LRU) % 2)
            outputs_hi_part(KD - 1, (KD - 1 + C_LRU) % 2)
            pool.wait_ge(r_te, 2)
            pool.dma_start(conv_prompt[0, 0], hrow[0:3, :]).then_inc(r_out, 16)
            pool.dma_start(conv_sample[0].rearrange("b j d -> (b j) d"), hrow[3:27, :]).then_inc(r_out, 16)
            pool.dma_start(h_prompt[0], hrow[27:28, :]).then_inc(r_out, 16)
            pool.dma_start(h_sample[0], hrow[28:36, :]).then_inc(r_out, 16)
            total(C_LO, 2)
            bias(2)
            total(C_FF1 + 26, 3)
            pool.wait_ge(r_out, 64)
            pool.wait_ge(s_lout[0], 96)
            pool.wait_ge(s_lout[1], 64)
            pool.wait_ge(s_lout[2], 32)


def constants():
    half = ROPE // 2
    freqs = np.float32(10000.0) ** (-np.arange(half, dtype=np.float32) / np.float32(half))
    pos = np.concatenate([np.arange(NP), np.tile(PAST + np.arange(TS), B)]).astype(np.float32)
    ang = (pos[:, None] * freqs[None, :]).astype(np.float32)
    cos, sin = np.cos(ang).T, np.sin(ang).T
    rot = np.concatenate([cos, cos, -sin, sin], axis=0)
    trig = np.concatenate([rot, rot * np.float32(SCALE)], axis=0).astype(np.float32)
    q, k = np.arange(P)[:, None], np.arange(P)[None, :]
    mask = np.where(k > q, np.float32(NEG), np.float32(0)).astype(np.float32)
    rows = np.arange(P)[:, None, None] % TS
    own = np.arange(B)[None, :, None]
    new = np.arange(NS)[None, None, :]
    seen = (new // TS == own) & (new % TS <= rows)
    smask = np.where(seen, np.float32(0), np.float32(NEG)).astype(np.float32).reshape(P, B * NS)
    return {"c_ident": np.eye(P, dtype=np.float32), "c_trig": trig, "c_mask": mask, "c_smask": smask}


_INS = ["x_prompt", "x_sample", "cache_latent", "cache_krope", "page_table", "state_lru_h", "state_conv",
        "meta_tokens", "mla_w_in", "mla_q_norm", "mla_w_q_up", "mla_kv_norm", "mla_w_uk", "mla_w_uv", "mla_w_o",
        "lru_w_in", "lru_conv_w", "lru_conv_b", "lru_w_a", "lru_b_a", "lru_w_i", "lru_b_i", "lru_lambda", "lru_w_o",
        "ffn_w_gu", "ffn_w_down", "ln_g", "ln_b"]
_OUTS = [(1, SEQ, D), (B, TS, D), (1, 1, NP, KV_R), (1, 1, NP, ROPE), (1, B, TS, KV_R), (1, B, TS, ROPE),
         (1, 1, D), (1, 1, CONV - 1, D), (1, B, D), (1, B, CONV - 1, D)]


def kernel(**inputs):
    import concourse.bacc as _bacc
    from concourse.bass_utils import run_bass_kernel_spmd as _run

    nc = _bacc.Bacc("TRN2", target_bir_lowering=False, num_devices=1)
    arrays, args = {}, []
    for name in _INS:
        arrays[f"in_{name}"] = np.ascontiguousarray(inputs[name])
    for name, a in constants().items():
        arrays[f"in_{name}"] = a
    for name, a in arrays.items():
        args.append(nc.dram_tensor(name, a.shape, mybir.dt.from_np(a.dtype), kind="ExternalInput").ap())
    for i, shape in enumerate(_OUTS):
        args.append(nc.dram_tensor(f"out_{i}", shape, F32, kind="ExternalOutput").ap())
    trunk(nc, *args)
    r = _run(nc, [arrays], core_ids=[0])
    return tuple(r.results[0][f"out_{i}"] for i in range(len(_OUTS)))
```
